# Optimizing a Trainium2 kernel written in Bass

```python
import jax, jax.numpy as jnp
from jax import lax
import numpy as np

D_MODEL = 1024
BATCH = 1
SEQ = 2048
DEPTH = 1
DEC_BATCH = 1
DEC_SEQ = 64
PAST_LEN = 128

CHUNK = 64
MIX_WIDTH = D_MODEL
ATTN_WIDTH = MIX_WIDTH // 2
POOL_WIDTH = MIX_WIDTH - ATTN_WIDTH
HEAD_DIM = 64
N_HEADS = ATTN_WIDTH // HEAD_DIM
POOL_WINDOWS = (2, 4, 8, 16)
N_POOL_GROUPS = len(POOL_WINDOWS)
POOL_GROUP = POOL_WIDTH // N_POOL_GROUPS
POOL_HIST = max(POOL_WINDOWS) - 1
Q_BLOCK = 128
EPS = 1e-6
IN_COLS = 4 * ATTN_WIDTH + N_HEADS + 2 * POOL_WIDTH

kernel_name = "fox_pool_hybrid_stream_step"

def rmsnorm(x, g):
    xf = x.astype(jnp.float32)
    y = xf * lax.rsqrt(jnp.mean(xf * xf, axis=-1, keepdims=True) + EPS)
    return (y * g.astype(jnp.float32)).astype(x.dtype)

def ada_terms(c, w_ada, b_ada):
    m = jax.nn.silu(c) @ w_ada + b_ada
    shift, scale, gate = jnp.split(m, 3, axis=-1)
    return shift, scale, gate

def project(x, c, norm_g, w_ada, b_ada, w_in, b_f):
    shift, scale, gate = ada_terms(c, w_ada, b_ada)
    h = rmsnorm(x, norm_g) * (1.0 + scale[:, None, :]) + shift[:, None, :]
    p = h @ w_in
    B, L, _ = p.shape
    A = ATTN_WIDTH
    q = p[..., 0:A].reshape(B, L, N_HEADS, HEAD_DIM)
    k = p[..., A:2 * A].reshape(B, L, N_HEADS, HEAD_DIM)
    v = p[..., 2 * A:3 * A].reshape(B, L, N_HEADS, HEAD_DIM)
    ag = p[..., 3 * A:4 * A]
    o = 4 * A
    logf = jax.nn.log_sigmoid(p[..., o:o + N_HEADS].astype(jnp.float32) + b_f.astype(jnp.float32))
    o += N_HEADS
    u = p[..., o:o + POOL_WIDTH]
    pg = p[..., o + POOL_WIDTH:o + 2 * POOL_WIDTH]
    return q, k, v, ag, logf, u, pg, gate

def fox_prompt(q, k, v, logf):
    B, L, H, dh = q.shape
    nb = L // Q_BLOCK
    Ft = jnp.cumsum(logf, axis=1).transpose(0, 2, 1)
    qb = q.reshape(B, nb, Q_BLOCK, H, dh).transpose(1, 0, 2, 3, 4)
    Fb = Ft.reshape(B, H, nb, Q_BLOCK).transpose(2, 0, 1, 3)
    kpos = jnp.arange(L)
    sc = 1.0 / np.sqrt(dh).astype(np.float32)

    def blk(args):
        qi, Fi, i = args
        qpos = i * Q_BLOCK + jnp.arange(Q_BLOCK)
        s = jnp.einsum('bqhd,bkhd->bhqk', qi, k, preferred_element_type=jnp.float32) * sc
        s = s + (Fi[:, :, :, None] - Ft[:, :, None, :])
        s = jnp.where(kpos[None, :] <= qpos[:, None], s, -jnp.inf)
        pr = jax.nn.softmax(s, axis=-1)
        return jnp.einsum('bhqk,bkhd->bqhd', pr.astype(v.dtype), v)

    out = lax.map(blk, (qb, Fb, jnp.arange(nb)))
    return out.transpose(1, 0, 2, 3, 4).reshape(B, L, H * dh)

def fox_sample(q, k_new, v_new, logf_new, cache_k, cache_v, cache_logf):
    B, L, H, dh = q.shape
    P = cache_k.shape[1]
    k = jnp.concatenate([cache_k.astype(k_new.dtype), k_new], axis=1)
    v = jnp.concatenate([cache_v.astype(v_new.dtype), v_new], axis=1)
    lf = jnp.concatenate([cache_logf.astype(jnp.float32), logf_new], axis=1)
    Ft = jnp.cumsum(lf, axis=1).transpose(0, 2, 1)
    sc = 1.0 / np.sqrt(dh).astype(np.float32)
    s = jnp.einsum('bqhd,bkhd->bhqk', q, k, preferred_element_type=jnp.float32) * sc
    s = s + (Ft[:, :, P:, None] - Ft[:, :, None, :])
    qpos = P + jnp.arange(L)
    kpos = jnp.arange(P + L)
    s = jnp.where(kpos[None, :] <= qpos[:, None], s, -jnp.inf)
    pr = jax.nn.softmax(s, axis=-1)
    return jnp.einsum('bhqk,bkhd->bqhd', pr.astype(v.dtype), v).reshape(B, L, H * dh)

def pool_mix(u_ext, start_pos, w_pool, pool_scale):
    B, E, C = u_ext.shape
    L = E - POOL_HIST
    uf = u_ext.astype(jnp.float32)
    cs = jnp.concatenate([jnp.zeros((B, 1, C), jnp.float32), jnp.cumsum(uf, axis=1)], axis=1)
    hi = cs[:, POOL_HIST + 1:POOL_HIST + 1 + L]
    pos = start_pos + jnp.arange(L)
    means = []
    for g, w in enumerate(POOL_WINDOWS):
        sl = slice(g * POOL_GROUP, (g + 1) * POOL_GROUP)
        lo = cs[:, POOL_HIST + 1 - w:POOL_HIST + 1 - w + L, sl]
        cnt = jnp.minimum(pos + 1, w).astype(jnp.float32)[None, :, None]
        means.append((hi[..., sl] - lo) / cnt)
    d = (jnp.concatenate(means, axis=-1) - uf[:, POOL_HIST:]).astype(u_ext.dtype)
    d = d.reshape(B, L, N_POOL_GROUPS, POOL_GROUP)
    y = jnp.einsum('blgc,gcd->blgd', d, w_pool).reshape(B, L, C)
    return y * pool_scale

def merge(x, attn, ag, pool, pg, gate, w_out):
    z = jnp.concatenate([attn * jax.nn.silu(ag), pool * jax.nn.silu(pg)], axis=-1)
    return x + gate[:, None, :] * (z @ w_out)

def setup_inputs(seed: int = 0) -> dict:
    key = jax.random.key(seed)
    ks = jax.random.split(key, 20)
    f32 = jnp.float32
    D = D_MODEL
    nrm = lambda k, s: jax.random.normal(k, s, f32)
    return {
        "x_prompt": nrm(ks[0], (BATCH, SEQ, D)),
        "x_sample": nrm(ks[1], (DEC_BATCH, DEC_SEQ, D)),
        "c_prompt": nrm(ks[2], (BATCH, D)),
        "c_sample": nrm(ks[3], (DEC_BATCH, D)),
        "cache_k": nrm(ks[4], (DEPTH, DEC_BATCH, PAST_LEN, N_HEADS, HEAD_DIM)),
        "cache_v": nrm(ks[5], (DEPTH, DEC_BATCH, PAST_LEN, N_HEADS, HEAD_DIM)),
        "cache_logf": jax.nn.log_sigmoid(nrm(ks[6], (DEPTH, DEC_BATCH, PAST_LEN, N_HEADS)) + 2.0),
        "state_pool": nrm(ks[7], (DEPTH, DEC_BATCH, POOL_HIST, POOL_WIDTH)),
        "norm_g": 1.0 + 0.05 * nrm(ks[8], (DEPTH, D)),
        "w_ada": 0.3 * D ** -0.5 * nrm(ks[9], (DEPTH, D, 3 * D)),
        "b_ada": 0.02 * nrm(ks[10], (DEPTH, 3 * D)),
        "w_in": D ** -0.5 * nrm(ks[11], (DEPTH, D, IN_COLS)),
        "b_f": 0.1 * nrm(ks[12], (DEPTH, N_HEADS)),
        "w_pool": POOL_GROUP ** -0.5 * nrm(ks[13], (DEPTH, N_POOL_GROUPS, POOL_GROUP, POOL_GROUP)),
        "pool_scale": 1.0 + 0.1 * nrm(ks[14], (DEPTH, POOL_WIDTH)),
        "w_out": MIX_WIDTH ** -0.5 * nrm(ks[15], (DEPTH, MIX_WIDTH, D)),
        "final_g": 1.0 + 0.05 * nrm(ks[16], (D,)),
    }

def reference(x_prompt, x_sample, c_prompt, c_sample, cache_k, cache_v, cache_logf, state_pool,
              norm_g, w_ada, b_ada, w_in, b_f, w_pool, pool_scale, w_out, final_g):
    xp, xs = x_prompt, x_sample
    past = cache_k.shape[2]
    kp_l, vp_l, fp_l, pp_l, ks_l, vs_l, fs_l, ps_l = [], [], [], [], [], [], [], []
    for l in range(DEPTH):
        q, k, v, ag, logf, u, pg, gate = project(xp, c_prompt, norm_g[l], w_ada[l], b_ada[l], w_in[l], b_f[l])
        attn = fox_prompt(q, k, v, logf)
        u_ext = jnp.pad(u, ((0, 0), (POOL_HIST, 0), (0, 0)))
        pool = pool_mix(u_ext, 0, w_pool[l], pool_scale[l])
        xp = merge(xp, attn, ag, pool, pg, gate, w_out[l])
        kp_l.append(k); vp_l.append(v); fp_l.append(logf); pp_l.append(u_ext[:, -POOL_HIST:])

        q, k, v, ag, logf, u, pg, gate = project(xs, c_sample, norm_g[l], w_ada[l], b_ada[l], w_in[l], b_f[l])
        attn = fox_sample(q, k, v, logf, cache_k[l], cache_v[l], cache_logf[l])
        u_ext = jnp.concatenate([state_pool[l].astype(u.dtype), u], axis=1)
        pool = pool_mix(u_ext, past, w_pool[l], pool_scale[l])
        xs = merge(xs, attn, ag, pool, pg, gate, w_out[l])
        ks_l.append(k); vs_l.append(v); fs_l.append(logf); ps_l.append(u_ext[:, -POOL_HIST:])

    y_prompt = rmsnorm(xp, final_g)
    y_sample = rmsnorm(xs, final_g)
    k_prompt = jnp.stack(kp_l); v_prompt = jnp.stack(vp_l)
    logf_prompt = jnp.stack(fp_l); pool_prompt = jnp.stack(pp_l)
    k_sample = jnp.stack(ks_l); v_sample = jnp.stack(vs_l)
    logf_sample = jnp.stack(fs_l); pool_sample = jnp.stack(ps_l)
    return (y_prompt, y_sample, k_prompt, v_prompt, logf_prompt, pool_prompt,
            k_sample, v_sample, logf_sample, pool_sample)


_drawn_inputs = setup_inputs


def setup_inputs(seed=0):
    import zlib

    import numpy as np

    out = dict(_drawn_inputs(seed))
    spreads = {}
    factors = {'cache_k': 8.0, 'cache_v': 8.0, 'cache_logf': 8.0, 'state_pool': 8.0, 'pool_scale': 7.873}
    for name, (base, spread) in spreads.items():
        noise = np.random.default_rng([zlib.crc32(name.encode()), seed]).standard_normal(out[name].shape)
        drawn = base * np.exp(spread * noise) if base else spread * noise
        out[name] = __import__('jax').numpy.asarray(drawn.astype(out[name].dtype))
    for name, factor in factors.items():
        out[name] = (out[name] * factor).astype(out[name].dtype)
    return out
```

```python
from contextlib import ExitStack

import concourse.bass as bass
from concourse import mybir

F32 = mybir.dt.float32
F32R = mybir.dt.float32r
BF16 = mybir.dt.bfloat16
ALU = mybir.AluOpType
ACT = mybir.ActivationFunctionType
AX = mybir.AxisListType.X

P = 128
D = 1024
KT = D // P
SEQ = 2048
DEC = 64
PAST = 128
HEADS = 8
DH = 64
PAIRS = HEADS // 2
GROUPS = 4
WINDOWS = (2, 4, 8, 16)
HIST = 15
A = 512
T = SEQ + DEC
TC = T + PAST
NQ = SEQ // P
EPS = 1e-6
SCALE = 1.0 / 8.0
MASKED = -1e30
CHUNKS = [(0, 512), (512, 512), (1024, 512), (1536, 288), (1824, 288)]
NCH = len(CHUNKS)
COL_Q, COL_K, COL_V, COL_AG, COL_F = 0, A, 2 * A, 3 * A, 4 * A
COL_U = COL_F + HEADS
COL_PG = COL_U + A
ROW_CP, ROW_CS, ROW_G, ROW_B, ROW_PS, NROWS = 0, 8, 16, 24, 48, 52


class Scope(ExitStack):

    def __init__(self, nc, tag):
        super().__init__()
        self.nc, self.tag = nc, tag

    def sb(self, name, shape, dt=F32):
        return self.enter_context(self.nc.sbuf_tensor(f"{self.tag}_{name}", shape, dt))

    def ps(self, name, shape, dt=F32):
        return self.enter_context(self.nc.psum_tensor(f"{self.tag}_{name}", shape, dt))

    def sem(self, name):
        return self.enter_context(self.nc.semaphore(f"{self.tag}_{name}"))


def raw(x):
    return x.bitcast(F32)


def stage_ada(nc, io, keep):
    with Scope(nc, "ada") as s:
        w = s.sb("w", [P, KT, 3 * D])
        rows = s.sb("rows", [NROWS, P])
        sc = s.sb("silu", [P, 2 * KT])
        mrow = s.sb("mrow", [2, 2 * D])
        one_b = s.sb("one_b", [P, 24])
        gate_b = s.sb("gate_b", [2, D])
        acc = [s.ps(f"acc{n}", [P, 512]) for n in range(6)]
        tps = s.ps("tps", [P, 512])
        cps = s.ps("cps", [P, 512])
        rows_in = s.sem("rows_in")
        w_in = [s.sem(f"w_in{k}") for k in range(KT)]
        g_in = s.sem("g_in")
        gb_in = s.sem("gb_in")
        const = s.sem("const")
        turned = s.sem("turned")
        cols_ok = s.sem("cols_ok")
        silu_ok = s.sem("silu_ok")
        m_full = s.sem("m_full")
        m_row = s.sem("m_row")
        m_col = s.sem("m_col")
        ab = s.sem("ab")
        cols, ident = keep["cols"], keep["ident"]
        wv = io["w_ada"][0].rearrange("(k p) n -> p k n", p=P)
        block = s.enter_context(nc.Block())

        @block.sync
        def _(sp):
            for k in range(KT):
                sp.dma_start(w[:, k, 0:2 * D], wv[:, k, 0:2 * D]).then_inc(w_in[k], 16)
            sp.dma_start(w[:, :, 2 * D:], wv[:, :, 2 * D:]).then_inc(g_in, 16)
            sp.dma_start(gate_b[:, :], io["b_ada"][:, 2 * D:].partition_broadcast(2)).then_inc(gb_in, 16)

        @block.scalar
        def _(act):
            small = [("c_prompt", ROW_CP, KT), ("c_sample", ROW_CS, KT), ("norm_g", ROW_G, KT),
                     ("b_ada", ROW_B, 24), ("pool_scale", ROW_PS, GROUPS)]
            for name, r, n in small:
                act.dma_start(rows[r:r + n, :], io[name].rearrange("a (k p) -> (a k) p", p=P)).then_inc(rows_in, 16)
            act.dma_start(keep["bf"][:, :], io["b_f"].rearrange("a h -> h a")).then_inc(rows_in, 16)
            act.wait_ge(cols_ok, 1)
            act.activation(sc[:, :], cols[:, ROW_CP:ROW_CP + 2 * KT], ACT.Silu).then_inc(silu_ok, 1)
            act.wait_ge(m_full, 1)
            for n in range(4):
                act.activation(mrow[:, n * 512:(n + 1) * 512], acc[n][0:2, :], ACT.Copy).then_inc(m_row, 1)
            act.wait_ge(rows_in, 96)
            act.wait_ge(m_row, 4)

        @block.gpsimd
        def _(pool):
            pool.memset(ident[:, :], 0.0).then_inc(const, 1)
            pool.memset(keep["mask"][:, :], 0.0).then_inc(const, 1)
            pool.wait_ge(const, 2)
            pool.affine_select(out=ident[:, :], in_=ident[:, :], compare_op=ALU.not_equal, fill=1.0, base=0,
                               pattern=[[-1, P]], channel_multiplier=1).then_inc(const, 1)
            pool.affine_select(out=keep["mask"][:, :], in_=keep["mask"][:, :], compare_op=ALU.is_ge, fill=MASKED,
                               base=0, pattern=[[-1, P]], channel_multiplier=1).then_inc(const, 1)
            pool.wait_ge(const, 4)
            pool.tensor_copy(keep["identb"][:, :], ident[:, :]).then_inc(const, 1)
            pool.wait_ge(const, 5)

        @block.tensor
        def _(pe):
            pe.wait_ge(rows_in, 96)
            pe.wait_ge(const, 3)
            pe.transpose(tps[:, 0:NROWS], rows[:, :], ident[0:NROWS, 0:NROWS]).then_inc(turned, 1)
            pe.wait_ge(silu_ok, 1)
            pair = sc[:, :].rearrange("p (w k) -> p k w", w=2)
            for k in range(KT):
                pe.wait_ge(w_in[k], 16)
                for n in range(4):
                    mm = pe.matmul(acc[n][0:2, :], pair[:, k, :], w[:, k, n * 512:(n + 1) * 512],
                                   start=(k == 0), stop=(k == KT - 1))
            mm.then_inc(m_full, 1)
            pe.wait_ge(m_row, 4)
            for n in range(2 * KT):
                mm = pe.transpose(cps[:, 2 * n:2 * n + 2], mrow[:, n * P:(n + 1) * P], ident[0:2, 0:2])
            mm.then_inc(m_col, 1)
            pe.wait_ge(g_in, 16)
            for k in range(KT):
                for n in range(2):
                    mm = pe.matmul(acc[4 + n][0:2, :], pair[:, k, :], w[:, k, 2 * D + n * 512:2 * D + (n + 1) * 512],
                                   start=(k == 0), stop=(k == KT - 1))
            mm.then_inc(m_full, 1)

        @block.vector
        def _(dve):
            dve.wait_ge(turned, 1)
            dve.tensor_copy(cols[:, :], tps[:, 0:NROWS]).then_inc(cols_ok, 1)
            dve.wait_ge(cols_ok, 1)
            dve.tensor_scalar(one_b[:, :], cols[:, ROW_B:ROW_B + 24], 1.0, None, ALU.add).then_inc(ab, 1)
            dve.wait_ge(m_col, 1)
            dve.wait_ge(ab, 1)
            for k in range(KT):
                dve.tensor_scalar(keep["shift"][:, k, :], cps[:, 2 * k:2 * k + 2],
                                  cols[:, ROW_B + k:ROW_B + k + 1], None, ALU.add).then_inc(ab, 1)
                dve.tensor_scalar(keep["scale"][:, k, :], cps[:, 2 * (KT + k):2 * (KT + k) + 2],
                                  one_b[:, KT + k:KT + k + 1], cols[:, ROW_G + k:ROW_G + k + 1],
                                  ALU.add, ALU.mult).then_inc(ab, 1)
            dve.wait_ge(m_full, 2)
            dve.wait_ge(gb_in, 16)
            for n in range(2):
                cs = slice(n * 512, (n + 1) * 512)
                dve.tensor_tensor(keep["gate"][:, cs], acc[4 + n][0:2, :], gate_b[:, cs], ALU.add).then_inc(ab, 1)
            dve.wait_ge(ab, 1 + 2 * KT + 2)


def stage_project(nc, io, keep, dram):
    with Scope(nc, "prj") as s:
        hhi = s.sb("hhi", [P, KT, T], F32R)
        hlo = s.sb("hlo", [P, KT, T], F32R)
        sv = Scope(nc, "prv")
        stage_values(nc, io, keep, dram, hhi, hlo, sv)
        stage_tiles(nc, io, keep, dram, hhi, hlo)


def stage_values(nc, io, keep, dram, hhi, hlo, s):
    NT = SEQ // P + 1
    with s:
        wraw = s.sb("wraw", [P, 2, 512])
        vhi_w = s.sb("vhi_w", [P, KT, 512], F32R)
        vlo_w = s.sb("vlo_w", [P, KT, 512], F32R)
        xt = s.sb("xt", [P, 2, D])
        xn = s.sb("xn", [P, D])
        hf = s.sb("hf", [P, D])
        vf = s.sb("vf", [P, 2, 512])
        vs = s.sb("vs", [P, 2, HEADS, P], F32R)
        st = s.sb("st", [P, 6, NT])
        xps = [s.ps(f"xps{n}", [P, D]) for n in range(2)]
        vps = [s.ps(f"vps{n}", [P, 512]) for n in range(2)]
        wr_in = [s.sem(f"wr_in{n}") for n in range(2)]
        w_hi, w_lo = s.sem("w_hi"), s.sem("w_lo")
        x_in = [s.sem(f"x_in{n}") for n in range(2)]
        sq, var, rs, nr, xn_ok = s.sem("sq"), s.sem("var"), s.sem("rs"), s.sem("nr"), s.sem("xn_ok")
        xturn, hf_ok, hi_ok, lo_ok = s.sem("xturn"), s.sem("hf_ok"), s.sem("hi_ok"), s.sem("lo_ok")
        v_full, vf_ok, vhi_ok, vlo_ok = s.sem("v_full"), s.sem("vf_ok"), s.sem("vhi_ok"), s.sem("vlo_ok")
        v_out = [s.sem(f"v_out{n}") for n in range(2)]
        vs_out = [s.sem(f"vs_out{n}") for n in range(2)]
        cv_in = s.sem("cv_in")
        block = s.enter_context(nc.Block())
        wv = io["w_in"][0].rearrange("(k p) n -> p k n", p=P)

        def rows_of(t):
            return P if t < NT - 1 else DEC

        def x_of(t):
            return io["x_prompt"][0, t * P:(t + 1) * P, :] if t < NT - 1 else io["x_sample"][0]

        def split_slots(t, even):
            v = vs[:, t % 2, :, :].rearrange("p (g e) c -> p g e c", e=2)
            return (v[:, :, 0, 0:DH], v[:, :, 1, DH:P]) if even else (v[:, :, 0, DH:P], v[:, :, 1, 0:DH])

        def heads(x):
            v = x.rearrange("p (g e d) -> p g e d", e=2, d=DH)
            return v[:, :, 0, :], v[:, :, 1, :]

        def store(sp, t):
            n = rows_of(t)
            sp.wait_ge(vf_ok, t + 1)
            dst = io["v_prompt"][0, 0, t * P:(t + 1) * P] if t < NT - 1 else io["v_sample"][0, 0]
            sp.dma_start(dst.rearrange("s h d -> s (h d)"), vf[0:n, t % 2, :]).then_inc(v_out[t % 2], 16)
            sp.wait_ge(vlo_ok, t + 1)
            sp.dma_start(dram["v"][t, 0:n, :], raw(vs[0:n, t % 2, :, :]).rearrange("p h c -> p (h c)")).then_inc(vs_out[t % 2], 16)

        def values(act, t, src, n, full):
            if full:
                act.wait_ge(v_full, t + 1)
                if t >= 2:
                    act.wait_ge(v_out[t % 2], 16 * (t // 2))
                act.activation(vf[0:n, t % 2, :], src, ACT.Copy).then_inc(vf_ok, 1)
            if t >= 2:
                act.wait_ge(vs_out[t % 2], 16 * (t // 2))
            for d, x in zip(split_slots(t, True), heads(src)):
                last = act.activation(d[0:n], x, ACT.Copy)
            last.then_inc(vhi_ok, 1)

        def lows(dve, t, src, n):
            dve.wait_ge(vhi_ok, t + 1)
            for d, x, hi in zip(split_slots(t, False), heads(src), split_slots(t, True)):
                last = dve.tensor_tensor(d[0:n], x, raw(hi[0:n]), ALU.subtract)
            last.then_inc(vlo_ok, 1)

        @block.sync
        def _(sp):
            for t in range(NT):
                n = rows_of(t)
                if t >= 2:
                    sp.wait_ge(xn_ok, t - 1)
                sp.dma_start(xt[0:n, t % 2, :], x_of(t)).then_inc(x_in[t % 2], 16)
                if t >= 2:
                    store(sp, t - 2)
            store(sp, NT - 2)
            store(sp, NT - 1)
            b = NT % 2
            sp.wait_ge(vlo_ok, NT - 1)
            sp.wait_ge(v_out[b], 16 * (NT // 2))
            sp.dma_start(vf[:, b, :], io["cache_v"][0, 0].rearrange("s h d -> s (h d)")).then_inc(cv_in, 16)
            sp.wait_ge(vhi_ok, NT + 1)
            sp.wait_ge(vlo_ok, NT + 1)
            sp.dma_start(dram["v"][NT, :, :], raw(vs[:, b, :, :]).rearrange("p h c -> p (h c)")).then_inc(vs_out[b], 16)
            for n in range(2):
                sp.wait_ge(v_out[n], 16 * len(range(n, NT, 2)))
                sp.wait_ge(vs_out[n], 16 * len(range(n, NT + 1, 2)))

        @block.scalar
        def _(act):
            for k in range(KT):
                if k >= 2:
                    act.wait_ge(w_lo, k - 1)
                act.dma_start(wraw[:, k % 2, :], wv[:, k, COL_V:COL_V + A]).then_inc(wr_in[k % 2], 16)

            def norm(t):
                n = rows_of(t)
                act.wait_ge(x_in[t % 2], 16 * (t // 2 + 1))
                if t >= 1:
                    act.wait_ge(xturn, t)
                act.activation(xn[0:n, :], xt[0:n, t % 2, :], ACT.Square, accum_out=st[0:n, 0, t:t + 1]).then_inc(sq, 1)
                act.wait_ge(var, 2 * t + 2)
                act.activation(st[0:n, 3, t:t + 1], st[0:n, 2, t:t + 1], ACT.Sqrt).then_inc(rs, 1)
                act.wait_ge(nr, 3 * t + 3)
                act.activation(xn[0:n, :], xt[0:n, t % 2, :], ACT.Copy, scale=st[0:n, 5, t:t + 1]).then_inc(xn_ok, 1)

            def high(t):
                n = rows_of(t)
                act.wait_ge(hf_ok, KT * (t + 1))
                act.activation(hhi[:, :, t * P:t * P + n], hf[:, :].rearrange("p (k c) -> p k c", k=KT)[:, :, 0:n],
                               ACT.Copy).then_inc(hi_ok, 1)

            norm(0)
            norm(1)
            high(0)
            for t in range(NT):
                if t + 2 < NT:
                    norm(t + 2)
                if t + 1 < NT:
                    high(t + 1)
                values(act, t, vps[t % 2][0:rows_of(t), :], rows_of(t), True)
            act.wait_ge(cv_in, 16)
            b = NT % 2
            values(act, NT, vf[:, b, :], P, False)

        @block.gpsimd
        def _(pool):
            for t in range(NT):
                n = rows_of(t)
                pool.wait_ge(hi_ok, t + 1)
                pool.tensor_tensor(hlo[:, :, t * P:t * P + n], hf[:, :].rearrange("p (k c) -> p k c", k=KT)[:, :, 0:n],
                                   raw(hhi[:, :, t * P:t * P + n]), ALU.subtract).then_inc(lo_ok, 1)

        @block.vector
        def _(dve):
            for k in range(KT):
                dve.wait_ge(wr_in[k % 2], 16 * (k // 2 + 1))
                dve.tensor_copy(vhi_w[:, k, :], wraw[:, k % 2, :]).then_inc(w_hi, 1)
                dve.wait_ge(w_hi, k + 1)
                dve.tensor_tensor(vlo_w[:, k, :], wraw[:, k % 2, :], raw(vhi_w[:, k, :]), ALU.subtract).then_inc(w_lo, 1)

            def stats(t):
                n = rows_of(t)
                dve.wait_ge(sq, t + 1)
                dve.tensor_scalar(st[0:n, 1, t:t + 1], st[0:n, 0, t:t + 1], 1.0 / D, EPS, ALU.mult, ALU.add).then_inc(var, 1)
                dve.wait_ge(var, 2 * t + 1)
                dve.reciprocal(st[0:n, 2, t:t + 1], st[0:n, 1, t:t + 1]).then_inc(var, 1)
                dve.wait_ge(rs, t + 1)
                dve.tensor_scalar(st[0:n, 4, t:t + 1], st[0:n, 3, t:t + 1], st[0:n, 3, t:t + 1], st[0:n, 1, t:t + 1],
                                  ALU.mult, ALU.mult).then_inc(nr, 1)
                dve.wait_ge(nr, 3 * t + 1)
                dve.tensor_scalar(st[0:n, 5, t:t + 1], st[0:n, 4, t:t + 1], -0.5, 1.5, ALU.mult, ALU.add).then_inc(nr, 1)
                dve.wait_ge(nr, 3 * t + 2)
                dve.tensor_scalar(st[0:n, 5, t:t + 1], st[0:n, 5, t:t + 1], st[0:n, 3, t:t + 1], None, ALU.mult).then_inc(nr, 1)

            def modulate(t):
                n = rows_of(t)
                which = 0 if t < NT - 1 else 1
                dve.wait_ge(xturn, t + 1)
                if t >= 1:
                    dve.wait_ge(lo_ok, t)
                for k in range(KT):
                    dve.tensor_scalar(hf[:, k * P:k * P + n], xps[t % 2][:, k * P:k * P + n],
                                      keep["scale"][:, k, which:which + 1], keep["shift"][:, k, which:which + 1],
                                      ALU.mult, ALU.add).then_inc(hf_ok, 1)

            stats(0)
            stats(1)
            modulate(0)
            for t in range(NT):
                if t + 2 < NT:
                    stats(t + 2)
                if t + 1 < NT:
                    modulate(t + 1)
                lows(dve, t, vps[t % 2][0:rows_of(t), :], rows_of(t))
            lows(dve, NT, vf[:, NT % 2, :], P)

        @block.tensor
        def _(pe):
            def turn(t):
                n = rows_of(t)
                pe.wait_ge(xn_ok, t + 1)
                if t >= 2:
                    pe.wait_ge(hf_ok, KT * (t - 1))
                for k in range(KT):
                    mm = pe.transpose(xps[t % 2][:, k * P:k * P + n], xn[0:n, k * P:(k + 1) * P], keep["ident"][0:n, 0:n])
                mm.then_inc(xturn, 1)

            turn(0)
            for t in range(NT):
                n = rows_of(t)
                if t + 1 < NT:
                    turn(t + 1)
                pe.wait_ge(lo_ok, t + 1)
                if t >= 2:
                    pe.wait_ge(vlo_ok, t - 1)
                cols = slice(t * P, t * P + n)
                for k in range(KT):
                    if t == 0:
                        pe.wait_ge(w_lo, k + 1)
                    pe.matmul(vps[t % 2][0:n, :], hhi[:, k, cols], vhi_w[:, k, :], start=(k == 0), stop=False)
                    pe.matmul(vps[t % 2][0:n, :], hhi[:, k, cols], vlo_w[:, k, :], start=False, stop=False)
                    mm = pe.matmul(vps[t % 2][0:n, :], hlo[:, k, cols], vhi_w[:, k, :], start=False, stop=(k == KT - 1))
                mm.then_inc(v_full, 1)


def stage_forget(nc, io, keep, dram, hhi, hlo, acc, full, free, spt):
    NF = SEQ // P + 2
    ODD = [1.0 / n for n in (15, 13, 11, 9, 7, 5, 3)]
    with Scope(nc, "fgt") as s:
        wfr = s.sb("wfr", [P, KT, HEADS])
        wf = s.sb("wf", [P, KT, DH], F32R)
        low = s.sb("low", [HEADS, TC])
        fx = s.sb("fx", [HEADS, TC])
        lx = s.sb("lx", [P, 6, (NF - 1) * HEADS])
        lf = s.sb("lf", [P, NF, HEADS])
        lft = s.sb("lft", [HEADS, TC])
        ones = s.sb("ones", [HEADS, TC])
        run = s.sb("run", [HEADS, TC])
        hi_r = s.sb("hi_r", [HEADS, TC], F32R)
        run_lo, neg_hi, neg_lo = low, fx, lft
        ck = s.sb("ck", [P, A])
        ckhi = s.sb("ckhi", [P, A], F32R)
        cklo = s.sb("cklo", [P, A], F32R)
        sp_rows = s.sb("sp_rows", [HIST, A])
        tps = s.ps("tps", [P, 512])
        kps = s.ps("kps", [P, 512])
        hps = s.ps("hps", [P, 512])
        w_in, c_in = s.sem("w_in"), s.sem("c_in")
        w_zero, w_hi, w_ok = s.sem("w_zero"), s.sem("w_hi"), s.sem("w_ok")
        low_ok, fturn, lx_ok, ex, lf_ok = s.sem("low_ok"), s.sem("fturn"), s.sem("lx_ok"), s.sem("ex"), s.sem("lf_ok")
        bturn, lft_ok, one_ok, run_ok, part_ok = s.sem("bturn"), s.sem("lft_ok"), s.sem("one_ok"), s.sem("run_ok"), s.sem("part_ok")
        cturn, ckhi_ok, cklo_ok, spt_ok = s.sem("cturn"), s.sem("ckhi_ok"), s.sem("cklo_ok"), s.sem("spt_ok")
        out = s.sem("out")
        block = s.enter_context(nc.Block())
        ident = keep["ident"]
        wv = io["w_in"][0].rearrange("(k p) n -> p k n", p=P)
        NM = (NF - 1) * HEADS

        @block.sync
        def _(sp):
            sp.dma_start(wfr[:, :, :], wv[:, :, COL_F:COL_F + HEADS]).then_inc(w_in, 16)
            sp.dma_start(ck[:, :], io["cache_k"][0, 0].rearrange("s h d -> s (h d)")).then_inc(c_in, 16)
            sp.dma_start(sp_rows[:, :], io["state_pool"][0, 0]).then_inc(c_in, 16)
            sp.dma_start(lf[:, NF - 1, :], io["cache_logf"][0, 0]).then_inc(c_in, 16)
            sp.wait_ge(ckhi_ok, 1)
            sp.dma_start(dram["k"][:, 0, :, T:TC].rearrange("g p c -> p g c"),
                         raw(ckhi[:, :]).rearrange("p (g c) -> p g c", g=PAIRS)).then_inc(out, 16)
            sp.wait_ge(cklo_ok, 1)
            sp.dma_start(dram["k"][:, 1, :, T:TC].rearrange("g p c -> p g c"),
                         raw(cklo[:, :]).rearrange("p (g c) -> p g c", g=PAIRS)).then_inc(out, 16)
            sp.wait_ge(lf_ok, 1)
            sp.dma_start(io["logf_prompt"][0, 0].rearrange("(t p) h -> p t h", p=P), lf[:, 0:NQ, :]).then_inc(out, 16)
            sp.dma_start(io["logf_sample"][0, 0], lf[0:DEC, NQ, :]).then_inc(out, 16)
            sp.wait_ge(part_ok, 3)
            hi = raw(hi_r[:, :])
            for r, (q, k) in enumerate([(hi, ones), (ones, neg_hi), (run_lo, ones), (ones, neg_lo)]):
                sp.dma_start(dram["fq"][:, r, :], q[:, :]).then_inc(out, 16)
                sp.dma_start(dram["fk"][:, r, :], k[:, :]).then_inc(out, 16)
            sp.wait_ge(out, 16 * 12)

        @block.gpsimd
        def _(pool):
            pool.memset(raw(wf[:, :, :]), 0.0).then_inc(w_zero, 1)
            pool.memset(ones[:, :], 1.0).then_inc(one_ok, 1)

        @block.scalar
        def _(act):
            for c, (c0, n) in enumerate(CHUNKS):
                act.wait_ge(full, c + 1)
                act.activation(low[:, c0:c0 + n], acc[c][32:32 + HEADS, 0:n], ACT.Copy).then_inc(low_ok, 1)
            act.wait_ge(cturn, 1)
            act.activation(ckhi[:, :], kps[:, :], ACT.Copy).then_inc(ckhi_ok, 1)
            act.wait_ge(cturn, 2)
            act.activation(spt[:, :, :], hps[:, 0:GROUPS * 16].rearrange("p (g c) -> p g c", c=16)[:, :, 0:HIST],
                           ACT.Copy).then_inc(spt_ok, 1)
            act.wait_ge(lx_ok, 4)
            act.activation(lx[:, 2, :], lx[:, 1, :], ACT.Exp, scale=-1.0).then_inc(ex, 1)
            for b in range(NCH):
                n = 512 if b < 4 else DEC + PAST
                act.wait_ge(bturn, b + 1)
                act.activation(lft[:, b * 512:b * 512 + n], acc[b][0:HEADS, 0:n], ACT.Copy).then_inc(lft_ok, 1)
            act.wait_ge(lft_ok, NCH)
            act.wait_ge(spt_ok, 1)

        @block.tensor
        def _(pe):
            pe.wait_ge(w_ok, 1)
            for c, (c0, n) in enumerate(CHUNKS):
                for k in range(KT):
                    for h in (hhi, hlo):
                        mm = pe.matmul(acc[c][0:DH, 0:n], wf[:, k, :], h[:, k, c0:c0 + n],
                                       start=(k == 0 and h is hhi), stop=(k == KT - 1 and h is hlo))
                mm.then_inc(full, 1)
            pe.wait_ge(c_in, 48)
            for g in range(PAIRS):
                mm = pe.transpose(kps[:, g * P:(g + 1) * P], ck[:, g * P:(g + 1) * P], ident[:, :])
            mm.then_inc(cturn, 1)
            for g in range(GROUPS):
                mm = pe.transpose(hps[:, 16 * g:16 * g + HIST], sp_rows[:, g * P:(g + 1) * P], ident[0:HIST, 0:HIST])
            mm.then_inc(cturn, 1)
            pe.wait_ge(free, NCH)
            for t in range(NF - 1):
                n = min(P, T - t * P)
                mm = pe.transpose(tps[0:n, t * HEADS:(t + 1) * HEADS], fx[:, t * P:t * P + n], ident[0:HEADS, 0:HEADS])
            mm.then_inc(fturn, 1)
            pe.wait_ge(lf_ok, 1)
            for t in range(NF):
                n = DEC if t == NF - 2 else P
                b = min(t // 4, 4)
                c = t * P - b * 512 if t < NF - 1 else DEC
                mm = pe.transpose(acc[b][0:HEADS, c:c + n], lf[0:n, t, :], ident[0:n, 0:n])
                if t % 4 == 3 or t == NF - 1:
                    mm.then_inc(bturn, 1)

        @block.vector
        def _(dve):
            dve.wait_ge(w_in, 16)
            dve.wait_ge(w_zero, 1)
            dve.tensor_copy(wf[:, :, 0:HEADS], wfr[:, :, :]).then_inc(w_hi, 1)
            dve.wait_ge(w_hi, 1)
            dve.tensor_tensor(wf[:, :, 32:32 + HEADS], wfr[:, :, :], raw(wf[:, :, 0:HEADS]), ALU.subtract).then_inc(w_ok, 1)
            for c, (c0, n) in enumerate(CHUNKS):
                dve.wait_ge(low_ok, c + 1)
                dve.scalar_tensor_tensor(out=fx[:, c0:c0 + n], in0=acc[c][0:HEADS, 0:n], scalar=keep["bf"][:, 0:1],
                                         in1=low[:, c0:c0 + n], op0=ALU.add, op1=ALU.add).then_inc(free, 1)
            dve.wait_ge(ckhi_ok, 1)
            dve.tensor_tensor(cklo[:, :], kps[:, :], raw(ckhi[:, :]), ALU.subtract).then_inc(cklo_ok, 1)
            x, ax, e, sq, q, mn = (lx[:, i, :] for i in range(6))
            dve.memset(x, 0.0).then_inc(lx_ok, 1)
            dve.wait_ge(lx_ok, 1)
            dve.wait_ge(fturn, 1)
            dve.tensor_copy(lx[:, 0, 0:NQ * HEADS], tps[:, 0:NQ * HEADS]).then_inc(lx_ok, 1)
            dve.tensor_copy(lx[0:DEC, 0, NQ * HEADS:NM], tps[0:DEC, NQ * HEADS:NM]).then_inc(lx_ok, 1)
            dve.wait_ge(lx_ok, 3)
            dve.scalar_tensor_tensor(out=ax, in0=x, scalar=-1.0, in1=x, op0=ALU.mult, op1=ALU.max).then_inc(lx_ok, 1)
            dve.tensor_scalar(mn, x, 0.0, None, ALU.min).then_inc(lx_ok, 1)
            dve.wait_ge(ex, 1)
            count = 5

            def step(ins):
                nonlocal count
                count += 1
                ins.then_inc(lx_ok, 1)
                dve.wait_ge(lx_ok, count)

            step(dve.tensor_scalar(q, e, 2.0, None, ALU.add))
            step(dve.reciprocal(ax, q))
            step(dve.tensor_tensor(e, e, ax, ALU.mult))
            step(dve.tensor_tensor(sq, e, e, ALU.mult))
            step(dve.tensor_scalar(q, sq, 1.0 / 17, None, ALU.mult))
            for c in ODD:
                step(dve.scalar_tensor_tensor(out=q, in0=q, scalar=c, in1=sq, op0=ALU.add, op1=ALU.mult))
            step(dve.scalar_tensor_tensor(out=q, in0=q, scalar=1.0, in1=e, op0=ALU.add, op1=ALU.mult))
            dve.scalar_tensor_tensor(out=lf[:, 0:NF - 1, :], in0=q.rearrange("p (t h) -> p t h", h=HEADS), scalar=-2.0,
                                     in1=mn.rearrange("p (t h) -> p t h", h=HEADS), op0=ALU.mult, op1=ALU.add).then_inc(lf_ok, 1)
            dve.wait_ge(lft_ok, NCH)
            dve.wait_ge(one_ok, 1)
            dve.tensor_tensor_scan(run[:, 0:SEQ], ones[:, 0:SEQ], lft[:, 0:SEQ], 0.0, ALU.mult, ALU.add).then_inc(run_ok, 1)
            dve.tensor_tensor_scan(run[:, T:TC], ones[:, T:TC], lft[:, T:TC], 0.0, ALU.mult, ALU.add).then_inc(run_ok, 1)
            dve.wait_ge(run_ok, 2)
            dve.tensor_tensor_scan(run[:, SEQ:T], ones[:, SEQ:T], lft[:, SEQ:T], run[:, TC - 1:TC], ALU.mult,
                                   ALU.add).then_inc(run_ok, 1)
            dve.wait_ge(run_ok, 3)
            dve.tensor_copy(hi_r[:, :], run[:, :]).then_inc(run_ok, 1)
            dve.wait_ge(run_ok, 4)
            dve.tensor_tensor(run_lo[:, :], run[:, :], raw(hi_r[:, :]), ALU.subtract).then_inc(part_ok, 1)
            dve.tensor_scalar(neg_hi[:, :], raw(hi_r[:, :]), -1.0, None, ALU.mult).then_inc(part_ok, 1)
            dve.tensor_tensor(neg_lo[:, :], raw(hi_r[:, :]), run[:, :], ALU.subtract).then_inc(part_ok, 1)


def stage_tiles(nc, io, keep, dram, hhi, hlo):
    TILES = [base + i * P for base in (COL_U, COL_PG, COL_AG, COL_K, COL_Q) for i in range(4)]
    U0, PG0, AG0, K0, Q0 = 0, 4, 8, 12, 16
    PARTS = [(p * 512, 512) for p in range(4)] + [(SEQ, DEC)]
    with Scope(nc, "til") as s:
        acc = [s.ps(f"acc{c}", [P, 512]) for c in range(NCH)]
        full, free = s.sem("full"), s.sem("free")
        spt = s.sb("spt", [P, GROUPS, HIST])
        stage_forget(nc, io, keep, dram, hhi, hlo, acc, full, free, spt)
        with Scope(nc, "out") as o:
            wraw = o.sb("wraw", [P, KT, P])
            whi = [o.sb(f"whi{n}", [P, KT, P], F32R) for n in range(2)]
            wlo = [o.sb(f"wlo{n}", [P, KT, P], F32R) for n in range(2)]
            of = [o.sb(f"of{c}", [P, 512]) for c in range(NCH)]
            ohi = [o.sb(f"ohi{c}", [P, 512], F32R) for c in range(NCH)]
            olo = [o.sb(f"olo{c}", [P, 512], F32R) for c in range(NCH)]
            ub = o.sb("ub", [P, HIST + 512])
            sa = o.sb("sa", [P, HIST + 512])
            sb_ = o.sb("sb", [P, HIST + 512])
            dhi = o.sb("dhi", [P, 512], F32R)
            dlo = o.sb("dlo", [P, 512], F32R)
            early = o.sb("early", [P, GROUPS, HIST + 1])
            slot0 = o.sb("slot0", [P, 2])
            zeros = o.sb("zeros", [P, KT, P])
            w_in, w_hi, w_lo = o.sem("w_in"), o.sem("w_hi"), o.sem("w_lo")
            hi_ok = o.sem("hi_ok")
            out_f = [o.sem(f"out_f{c}") for c in range(NCH)]
            out_s = [o.sem(f"out_s{c}") for c in range(NCH)]
            u_in, u_out, pl, early_ok, dstep, zero_ok = o.sem("u_in"), o.sem("u_out"), o.sem("pl"), o.sem("early_ok"), o.sem("dstep"), o.sem("zero_ok")
            block = o.enter_context(nc.Block())
            wv = io["w_in"][0].rearrange("(k p) n -> p k n", p=P)

            @block.sync
            def _(sp):
                for n, col in enumerate(TILES):
                    if n >= 1:
                        sp.wait_ge(w_lo, n)
                    sp.dma_start(wraw[:, :, :], wv[:, :, col:col + P]).then_inc(w_in, 16)
                    for i in range(max(0, (n - 5) * 3), min(20, (n - 4) * 3)):
                        g, p = divmod(i, len(PARTS))
                        p0, w = PARTS[p]
                        for c in range(NCH):
                            sp.wait_ge(out_f[c], 16 * (g + 2))
                        if i >= 1:
                            sp.wait_ge(pl, i)
                        h = HIST if 0 < p < 4 else 0
                        sp.dma_start(ub[:, HIST - h:HIST + w], dram["u"][g, :, p0 - h:p0 + w]).then_inc(u_in, 16)
                        sp.wait_ge(pl, i + 1)
                        sp.dma_start(dram["d"][0, g, :, p0:p0 + w], raw(dhi[:, 0:w])).then_inc(u_out, 16)
                        sp.dma_start(dram["d"][1, g, :, p0:p0 + w], raw(dlo[:, 0:w])).then_inc(u_out, 16)
                sp.wait_ge(u_out, 32 * GROUPS * len(PARTS))

            @block.gpsimd
            def _(pool):
                pool.memset(zeros[:, :, :], 0.0).then_inc(zero_ok, 1)
                pool.wait_ge(zero_ok, 1)
                for c in range(NCH):
                    pool.memset(slot0[:, 0:1], 0.0).then_inc(out_f[c], 16)
                    pool.memset(slot0[:, 1:2], 0.0).then_inc(out_s[c], 32)
                    pool.wait_ge(out_f[c], 16)
                    pool.wait_ge(out_s[c], 32)
                for g, w in enumerate(WINDOWS):
                    for t in range(HIST + 1):
                        pool.memset(early[:, g, t:t + 1], w / min(t + 1, w)).then_inc(early_ok, 1)
                with pool.Fori(0, len(TILES) // 2) as m:
                    for b in range(2):
                        n = 2 * m + b
                        pool.wait_ge(w_in, 16 * n + 16)
                        pool.wait_ge(full, NCH * 2 * m + (1 if b == 0 else NCH))
                        pool.tensor_tensor(whi[b][:, :, :], wraw[:, :, :], zeros[:, :, :], ALU.add).then_inc(w_hi, 1)
                        pool.wait_ge(w_hi, n + 1)
                        pool.tensor_tensor(wlo[b][:, :, :], wraw[:, :, :], raw(whi[b][:, :, :]),
                                           ALU.subtract).then_inc(w_lo, 1)

            @block.tensor
            def _(pe):
                with pe.Fori(0, len(TILES) // 2) as m:
                    for b in range(2):
                        pe.wait_ge(w_lo, 2 * m + b + 1)
                        for c, (c0, n) in enumerate(CHUNKS):
                            pe.wait_ge(free, NCH * 2 * m + NCH * b + c + 1)
                            for k in range(KT):
                                pe.matmul(acc[c][:, 0:n], whi[b][:, k, :], hhi[:, k, c0:c0 + n], start=(k == 0), stop=False)
                                pe.matmul(acc[c][:, 0:n], wlo[b][:, k, :], hhi[:, k, c0:c0 + n], start=False, stop=False)
                                mm = pe.matmul(acc[c][:, 0:n], whi[b][:, k, :], hlo[:, k, c0:c0 + n],
                                               start=False, stop=(k == KT - 1))
                            mm.then_inc(full, 1)

            @block.scalar
            def _(act):
                def each_tile(first, body, stores):
                    with act.Fori(0, 4) as i:
                        for c in range(NCH + 1):
                            if c < NCH:
                                act.wait_ge(full, NCH * i + NCH * (first + 1) + c + 1)
                                body(i, c, CHUNKS[c][1])
                            if c >= 1:
                                act.wait_ge(free, NCH * i + NCH * (first + 1) + c)
                                stores(i, c - 1, *CHUNKS[c - 1])

                def plain(base, func):
                    def body(i, c, n):
                        act.wait_ge(out_f[c], 16 * i + 16 * (base + 1))
                        act.activation(of[c][:, 0:n], acc[c][:, 0:n], func).then_inc(free, 1)
                    return body

                def store_f(name):
                    def stores(i, c, c0, n):
                        act.dma_start(dram[name][i, :, c0:c0 + n], of[c][:, 0:n]).then_inc(out_f[c], 16)
                    return stores

                def split_k(i, c, n):
                    act.wait_ge(out_f[c], 16 * i + 16 * 13)
                    act.activation(of[c][:, 0:n], acc[c][:, 0:n], ACT.Copy)
                    act.wait_ge(out_s[c], 32 * i + 32)
                    act.activation(ohi[c][:, 0:n], acc[c][:, 0:n], ACT.Copy).then_inc(hi_ok, 1)

                def split_q(i, c, n):
                    act.wait_ge(out_s[c], 32 * i + 32 * 5)
                    act.activation(ohi[c][:, 0:n], acc[c][:, 0:n], ACT.Copy, scale=SCALE).then_inc(hi_ok, 1)

                def store_s(name, full_too):
                    def stores(i, c, c0, n):
                        act.dma_start(dram[name][i, 0, :, c0:c0 + n], raw(ohi[c][:, 0:n])).then_inc(out_s[c], 16)
                        act.dma_start(dram[name][i, 1, :, c0:c0 + n], raw(olo[c][:, 0:n])).then_inc(out_s[c], 16)
                        if full_too:
                            act.dma_start(dram["kf"][i, :, c0:c0 + n], of[c][:, 0:n]).then_inc(out_f[c], 16)
                    return stores

                each_tile(U0, plain(0, ACT.Copy), store_f("u"))
                each_tile(PG0, plain(4, ACT.Silu), store_f("pg"))
                each_tile(AG0, plain(8, ACT.Silu), store_f("ag"))
                each_tile(K0, split_k, store_s("k", True))
                each_tile(Q0, split_q, store_s("q", False))
                for c in range(NCH):
                    act.wait_ge(out_f[c], 16 * 17)
                    act.wait_ge(out_s[c], 32 * 9)

            @block.vector
            def _(dve):
                count = 0

                def step(ins):
                    nonlocal count
                    count += 1
                    ins.then_inc(dstep, 1)
                    dve.wait_ge(dstep, count)

                def pool_part(g, p, p0, w):
                    i = g * len(PARTS) + p
                    win = WINDOWS[g]
                    if p == 0:
                        step(dve.memset(ub[:, 0:HIST], 0.0))
                    if p == len(PARTS) - 1:
                        step(dve.tensor_copy(ub[:, 0:HIST], spt[:, g, :]))
                    dve.wait_ge(u_in, 16 * (i + 1))
                    src, n, end = ub, 1, HIST + w
                    bufs = [sa, sb_]
                    while n < win:
                        dst = bufs[0]
                        step(dve.tensor_tensor(dst[:, 2 * n - 1:end], src[:, 2 * n - 1:end], src[:, n - 1:end - n], ALU.add))
                        src, n, bufs = dst, 2 * n, bufs[::-1]
                    if p == 0:
                        step(dve.tensor_tensor(src[:, HIST:HIST + win - 1], src[:, HIST:HIST + win - 1],
                                               early[:, g, 0:win - 1], ALU.mult))
                    d = bufs[0][:, 0:w]
                    step(dve.scalar_tensor_tensor(out=d, in0=src[:, HIST:end], scalar=1.0 / win, in1=ub[:, HIST:end],
                                                  op0=ALU.mult, op1=ALU.subtract))
                    if i >= 1:
                        dve.wait_ge(u_out, 32 * i)
                    step(dve.tensor_copy(dhi[:, 0:w], d))
                    dve.tensor_tensor(dlo[:, 0:w], d, raw(dhi[:, 0:w]), ALU.subtract).then_inc(pl, 1)
                    dve.wait_ge(pl, i + 1)

                dve.wait_ge(early_ok, GROUPS * (HIST + 1))
                for g in range(GROUPS):
                    for p, (p0, w) in enumerate(PARTS):
                        pool_part(g, p, p0, w)
                for first, scale in ((K0, 1.0), (Q0, SCALE)):
                    with dve.Fori(0, 4) as i:
                        for c, (_, n) in enumerate(CHUNKS):
                            dve.wait_ge(hi_ok, NCH * i + NCH * (first - K0) + c + 1)
                            dve.scalar_tensor_tensor(out=olo[c][:, 0:n], in0=acc[c][:, 0:n], scalar=scale,
                                                     in1=raw(ohi[c][:, 0:n]), op0=ALU.mult, op1=ALU.subtract).then_inc(free, 1)


def stage_pool(nc, io, keep, dram):
    NT = NQ + 1
    with Scope(nc, "pol") as s:
        wp = s.sb("wp", [P, GROUPS, P])
        wphi = s.sb("wphi", [P, GROUPS, P], F32R)
        wplo = s.sb("wplo", [P, GROUPS, P], F32R)
        dh = s.sb("dh", [P, GROUPS, T], F32R)
        dl = s.sb("dl", [P, GROUPS, T], F32R)
        pg = s.sb("pg", [P, GROUPS, T])
        kf = s.sb("kf", [P, PAIRS, T])
        ul = s.sb("ul", [P, 2, GROUPS, HIST])
        zf = s.sb("zf", [P, 2, 512])
        zhi = s.sb("zhi", [P, 2, 512], F32R)
        zlo = s.sb("zlo", [P, 2, 512], F32R)
        krow = s.sb("krow", [P, 2, 512])
        urow = s.sb("urow", [HIST, 2, A])
        acc = [s.ps(f"acc{n}", [P, 512]) for n in range(2)]
        kps = [s.ps(f"kps{n}", [P, 512]) for n in range(2)]
        ups = [s.ps(f"ups{n}", [P, 512]) for n in range(2)]
        wp_in, ul_in = s.sem("wp_in"), s.sem("ul_in")
        d_in = [s.sem(f"d_in{g}") for g in range(GROUPS)]
        k_in = s.sem("k_in")
        w_hi, w_lo, full, zf_ok, zhi_ok, zlo_ok = (s.sem(n) for n in ("w_hi", "w_lo", "full", "zf_ok", "zhi_ok", "zlo_ok"))
        z_out = [s.sem(f"z_out{n}") for n in range(2)]
        k_out = [s.sem(f"k_out{n}") for n in range(2)]
        u_turn, u_row, u_out, k_turn, k_row = (s.sem(n) for n in ("u_turn", "u_row", "u_out", "k_turn", "k_row"))
        block = s.enter_context(nc.Block())
        ident = keep["ident"]
        WORK = [(g, c) for g in range(GROUPS) for c in range(NCH)]

        @block.sync
        def _(sp):
            sp.dma_start(wp[:, :, :], io["w_pool"][0].rearrange("g c d -> c g d")).then_inc(wp_in, 16)
            for g in range(GROUPS):
                sp.dma_start(raw(dh[:, g, :]), dram["d"][0, g]).then_inc(d_in[g], 16)
                sp.dma_start(raw(dl[:, g, :]), dram["d"][1, g]).then_inc(d_in[g], 16)
                sp.dma_start(pg[:, g, :], dram["pg"][g]).then_inc(d_in[g], 16)
            for i, (g, c) in enumerate(WORK):
                c0, n = CHUNKS[c]
                sp.wait_ge(zlo_ok, i + 1)
                for part, z in enumerate((zhi, zlo)):
                    sp.dma_start(dram["z"][part, PAIRS + g, :, c0:c0 + n], raw(z[:, i % 2, 0:n])).then_inc(z_out[i % 2], 16)
            for n in range(2):
                sp.wait_ge(z_out[n], 32 * len(WORK[n::2]))

        @block.scalar
        def _(act):
            for p in range(PAIRS):
                act.dma_start(kf[:, p, :], dram["kf"][p]).then_inc(k_in, 16)
            for n, end in enumerate((SEQ, T)):
                act.dma_start(ul[:, n, :, :], dram["u"][:, :, end - HIST:end].rearrange("g p c -> p g c")).then_inc(ul_in, 16)
            work = list(enumerate(WORK))
            for t in range(max(NT, len(work))):
                if t < len(work):
                    i, (g, c) = work[t]
                    n = CHUNKS[c][1]
                    act.wait_ge(zf_ok, i + 1)
                    if i >= 2:
                        act.wait_ge(z_out[i % 2], 32 * (i // 2))
                    act.activation(zhi[:, i % 2, 0:n], zf[:, i % 2, 0:n], ACT.Copy).then_inc(zhi_ok, 1)
                if t < NT:
                    n = P if t < NQ else DEC
                    act.wait_ge(k_turn, t + 1)
                    if t >= 2:
                        act.wait_ge(k_out[t % 2], 16 * (t // 2))
                    act.activation(krow[0:n, t % 2, :], kps[t % 2][0:n, :], ACT.Copy).then_inc(k_row, 1)
            for n in range(2):
                act.wait_ge(u_turn, n + 1)
                act.activation(urow[:, n, :], ups[n][0:HIST, :], ACT.Copy).then_inc(u_row, 1)
            act.wait_ge(u_row, 2)
            act.dma_start(io["pool_prompt"][0, 0], urow[:, 0, :]).then_inc(u_out, 16)
            act.dma_start(io["pool_sample"][0, 0], urow[:, 1, :]).then_inc(u_out, 16)
            act.wait_ge(u_out, 32)

        @block.gpsimd
        def _(pool):
            for t in range(NT):
                n = P if t < NQ else DEC
                dst = io["k_prompt"][0, 0, t * P:(t + 1) * P] if t < NQ else io["k_sample"][0, 0]
                pool.wait_ge(k_row, t + 1)
                pool.dma_start(dst.rearrange("s h d -> s (h d)"), krow[0:n, t % 2, :]).then_inc(k_out[t % 2], 16)
            for n in range(2):
                pool.wait_ge(k_out[n], 16 * len(range(n, NT, 2)))

        @block.tensor
        def _(pe):
            work = list(enumerate(WORK))
            pe.wait_ge(k_in, 64)
            for t in range(max(NT, len(work))):
                if t < NT:
                    n = P if t < NQ else DEC
                    if t >= 2:
                        pe.wait_ge(k_row, t - 1)
                    for p in range(PAIRS):
                        mm = pe.transpose(kps[t % 2][0:n, p * P:(p + 1) * P], kf[:, p, t * P:t * P + n], ident[:, :])
                    mm.then_inc(k_turn, 1)
                if t < len(work):
                    i, (g, c) = work[t]
                    c0, n = CHUNKS[c]
                    pe.wait_ge(w_lo, 1)
                    pe.wait_ge(d_in[g], 48)
                    if i >= 2:
                        pe.wait_ge(zf_ok, i - 1)
                    pe.matmul(acc[i % 2][:, 0:n], wphi[:, g, :], dh[:, g, c0:c0 + n], start=True, stop=False)
                    pe.matmul(acc[i % 2][:, 0:n], wplo[:, g, :], dh[:, g, c0:c0 + n], start=False, stop=False)
                    pe.matmul(acc[i % 2][:, 0:n], wphi[:, g, :], dl[:, g, c0:c0 + n], start=False, stop=True).then_inc(full, 1)
            pe.wait_ge(ul_in, 32)
            for n in range(2):
                for g in range(GROUPS):
                    mm = pe.transpose(ups[n][0:HIST, g * P:(g + 1) * P], ul[:, n, g, :], ident[:, :])
                mm.then_inc(u_turn, 1)

        @block.vector
        def _(dve):
            dve.wait_ge(wp_in, 16)
            dve.tensor_copy(wphi[:, :, :], wp[:, :, :]).then_inc(w_hi, 1)
            dve.wait_ge(w_hi, 1)
            dve.tensor_tensor(wplo[:, :, :], wp[:, :, :], raw(wphi[:, :, :]), ALU.subtract).then_inc(w_lo, 1)
            for i, (g, c) in enumerate(WORK):
                c0, n = CHUNKS[c]
                dve.wait_ge(full, i + 1)
                dve.wait_ge(d_in[g], 48)
                if i >= 2:
                    dve.wait_ge(zlo_ok, i - 1)
                dve.scalar_tensor_tensor(out=zf[:, i % 2, 0:n], in0=acc[i % 2][:, 0:n],
                                         scalar=keep["cols"][:, ROW_PS + g:ROW_PS + g + 1], in1=pg[:, g, c0:c0 + n],
                                         op0=ALU.mult, op1=ALU.mult).then_inc(zf_ok, 1)
                dve.wait_ge(zhi_ok, i + 1)
                dve.tensor_tensor(zlo[:, i % 2, 0:n], zf[:, i % 2, 0:n], raw(zhi[:, i % 2, 0:n]), ALU.subtract).then_inc(zlo_ok, 1)


class Row:

    def __init__(self, head, tile):
        self.head, self.tile = head, tile
        self.dec = tile == NQ
        self.m = DEC if self.dec else P
        self.q0 = tile * P
        keys = (tile + 1) * P
        self.chunks = [(SEQ, DEC + PAST)] if self.dec else [(k, min(512, keys - k)) for k in range(0, keys, 512)]
        self.mask0 = 0 if self.dec else (tile % 4) * P


class Plan:

    LEAD, LAG = 4, 2

    def __init__(self):
        self.units, self.rows, self.scores, self.groups = [], [], [], []
        for head in range(2):
            for tiles in [(2 * u, 2 * u + 1) for u in range(NQ // 2)] + [(NQ,)]:
                unit = {"n": len(self.units), "head": head, "rows": [], "groups": [], "scores": []}
                for t in tiles:
                    r = Row(head, t)
                    r.n, r.slot, r.unit = len(self.rows), len(unit["rows"]), unit
                    self.rows.append(r)
                    unit["rows"].append(r)
                    for c in range(len(r.chunks)):
                        unit["scores"].append((r, c))
                self.units.append(unit)
                for g in range(1 if tiles[0] == NQ else tiles[0] // 2 + 1):
                    unit["groups"].append({"unit": unit, "g": g, "last": g == tiles[0] // 2 or tiles[0] == NQ})
        for u in self.units:
            u["score0"] = len(self.scores)
            self.scores += u["scores"]
            u["score1"] = len(self.scores)
        self.events = []
        issued = 0
        waiting = []
        real = 0
        turned = 0

        def put_scores(upto):
            nonlocal issued
            while issued < min(upto, len(self.scores)):
                r, c = self.scores[issued]
                self.events.append(("score", issued, r, c))
                issued += 1

        def put_values():
            g = waiting.pop(0)
            self.events.append(("value", g))
            if g is g["unit"]["groups"][-1]:
                self.events.append(("out", g["unit"]))

        put_scores(self.units[0]["score1"])
        for u in self.units:
            nxt = self.units[u["n"] + 1] if u["n"] + 1 < len(self.units) else None
            for i, g in enumerate(u["groups"]):
                g["real"], g["turn"] = real, turned
                real, turned = real + 1, turned + 1
                self.events.append(("turn", g))
                waiting.append(g)
                if nxt:
                    n = nxt["score1"] - nxt["score0"]
                    limit = self.units[min(u["n"] + 2, len(self.units) - 1)]["score1"]
                    put_scores(min(limit, u["score1"] + -(-n * (i + 1) // len(u["groups"])) + self.LEAD))
                if len(waiting) > self.LAG:
                    put_values()
            u["turn_end"] = turned
            if u["n"] == len(self.units) // 2:
                self.events.append(("den", 0, turned))
                self.den = [turned]
                turned += 1
        while waiting:
            put_values()
        self.events.append(("den", 1, turned))
        self.den.append(turned)
        turned += 1
        self.n_turn, self.n_real = turned, real


def stage_attend(nc, io, keep, dram):
    plan = Plan()
    NS, NR, NU, NT, NG = len(plan.scores), len(plan.rows), len(plan.units), plan.n_turn, plan.n_real
    S_RING, T_RING, W_RING, O_RING, P_RING = 4, 2, 3, 2, 3
    multi = [r for r in plan.rows if len(r.chunks) > 1]
    NM = sum(len(r.chunks) for r in multi)
    mi = 0
    for r in multi:
        mi += len(r.chunks)
        r.max_end = mi
    RH = NR // 2

    def ring(k, size, per, j):
        return per * j + (size if k < size else k + 1)

    with Scope(nc, "att") as s:
        qa = [s.sb(f"qa{e}", [P, T], F32R) for e in range(2)]
        qb = [s.sb(f"qb{e}", [DH + 4, T], F32R) for e in range(2)]
        ka = [s.sb(f"ka{e}", [P, TC], F32R) for e in range(2)]
        kb = [s.sb(f"kb{e}", [DH + 4, TC], F32R) for e in range(2)]
        vt = [s.sb(f"vt{e}", [P, NQ + 2, P], F32R) for e in range(2)]
        w = [[s.sb(f"w{n}{r}", [P, SEQ]) for r in range(2)] for n in range(P_RING)]
        whi = [s.sb(f"whi{n}", [P, 512], F32R) for n in range(W_RING)]
        wlo = [s.sb(f"wlo{n}", [P, 512], F32R) for n in range(W_RING)]
        nmax = s.sb("nmax", [P, NR, 5])
        lsum = s.sb("lsum", [P, NR, 4])
        den = s.sb("den", [P, 2, 2, RH])
        rdt = s.sb("rdt", [RH, 2, P])
        tmp = s.sb("tmp", [P, 2, 256])
        att = s.sb("att", [P, T])
        zc = s.sb("zc", [P, 3, 512])
        zhi = s.sb("zhi", [P, 512], F32R)
        zlo = s.sb("zlo", [P, 512], F32R)
        zeros = s.sb("zeros", [P, 512])
        start = s.sb("start", [P, 8])
        sps = [s.ps(f"sps{n}", [P, 512]) for n in range(S_RING)]
        pps = [s.ps(f"pps{n}", [P, 512]) for n in range(T_RING)]
        ops = [s.ps(f"ops{n}", [P, 512]) for n in range(O_RING)]
        loaded = [s.sem(f"loaded{e}") for e in range(2)]
        ready, s_full, exp_ok, mx_part, mx = (s.sem(n) for n in ("ready", "s_full", "exp_ok", "mx_part", "mx"))
        turned, hi_ok, lo_ok, val_ok, low_out, out_ok = (s.sem(n) for n in ("turned", "hi_ok", "lo_ok", "val_ok", "low_out", "out_ok"))
        den_ok, zstep, zin, zout = (s.sem(n) for n in ("den_ok", "zstep", "zin", "zout"))
        block = s.enter_context(nc.Block())

        def pieces(g):
            if g["unit"]["rows"][0].dec:
                return [(P, 0, P + DEC)]
            return [(P, 0, 3 * P if g["last"] else 4 * P)]

        def halves(e):
            return (slice(0, DH), slice(DH, P)) if e == 0 else (slice(DH, P), slice(0, DH))

        def load(sp, j, e):
            lo, hi = e * DH, (e + 1) * DH
            h = 2 * j + e
            for dst, src in ((qa[e][0:DH, :], dram["q"][j, 0, lo:hi, :]), (qa[e][DH:P, :], dram["q"][j, 1, lo:hi, :]),
                             (qb[e][0:DH, :], dram["q"][j, 0, lo:hi, :]), (qb[e][DH:DH + 4, :], dram["fq"][h, :, 0:T]),
                             (ka[e][0:DH, :], dram["k"][j, 0, lo:hi, :]), (ka[e][DH:P, :], dram["k"][j, 0, lo:hi, :]),
                             (kb[e][0:DH, :], dram["k"][j, 1, lo:hi, :]), (kb[e][DH:DH + 4, :], dram["fk"][h, :, :])):
                sp.dma_start(raw(dst), src).then_inc(loaded[e], 16)
            v = dram["v"][:, :, bass.ts(h, P)]
            sp.dma_start(raw(vt[e][0:DEC, :, :]), v[:, 0:DEC].rearrange("t p c -> p t c")).then_inc(loaded[e], 16)
            for a, b in ((0, NQ), (NQ + 1, NQ + 2)):
                sp.dma_start(raw(vt[e][DEC:P, a:b, :]), v[a:b, DEC:P].rearrange("t p c -> p t c")).then_inc(loaded[e], 16)

        LOADED = 16 * 11
        Z0 = 4 * NCH + 4

        def gate(sp, j, e):
            rows, _ = halves(e)
            h = 2 * j + e
            IN, OUT = 32 + 32 * NCH, 32 * NCH
            sp.wait_ge(lo_ok, NT * j + plan.den[e] + 1 + T_RING)
            sp.dma_start(dram["rden"][h, 0:SEQ].rearrange("(t q) -> t q", q=P), rdt[0:NQ, e, :]).then_inc(zin, 16)
            sp.dma_start(dram["rden"][h, SEQ:T].rearrange("(t q) -> t q", q=DEC), rdt[NQ:NQ + 1, e, 0:DEC]).then_inc(zin, 16)
            sp.wait_ge(zin, IN * h + 32)
            for c, (c0, n) in enumerate(CHUNKS):
                sp.wait_ge(zstep, Z0 + 4 * NCH * h + 4 * c)
                sp.dma_start(zc[rows, 0, 0:n], dram["rden"][h, c0:c0 + n].partition_broadcast(DH)).then_inc(zin, 16)
                sp.dma_start(zc[rows, 1, 0:n], dram["ag"][j, rows, c0:c0 + n]).then_inc(zin, 16)
                sp.wait_ge(zstep, Z0 + 4 * NCH * h + 4 * c + 4)
                sp.dma_start(dram["z"][0, j, rows, c0:c0 + n], raw(zhi[rows, 0:n])).then_inc(zout, 16)
                sp.dma_start(dram["z"][1, j, rows, c0:c0 + n], raw(zlo[rows, 0:n])).then_inc(zout, 16)

        @block.sync
        def _(sp):
            load(sp, 0, 0)
            load(sp, 0, 1)
            sp.wait_ge(ready, 1)
            with sp.Fori(0, PAIRS - 1) as j:
                for e in range(2):
                    sp.wait_ge(val_ok, NG * j + (NG // 2) * (e + 1) + W_RING)
                    load(sp, j + 1, e)
                    gate(sp, j, e)
            for e in range(2):
                gate(sp, PAIRS - 1, e)
            sp.wait_ge(zout, 16 + 32 * NCH * HEADS)

        @block.tensor
        def _(pe):
            pe.wait_ge(ready, 1)
            with pe.Fori(0, PAIRS) as j:
                for ev in plan.events:
                    if ev[0] == "score":
                        _, k, r, c = ev
                        k0, n = r.chunks[c]
                        e = r.head
                        if r.tile == 0 and c == 0:
                            pe.wait_ge(loaded[e], LOADED * j + LOADED)
                        pe.wait_ge(exp_ok, ring(k, S_RING, NS, j))
                        out = sps[k % S_RING][0:r.m, 0:n]
                        last = c == len(r.chunks) - 1
                        pe.matmul(out, qa[e][:, r.q0:r.q0 + r.m], ka[e][:, k0:k0 + n], start=True, stop=False)
                        mm = pe.matmul(out, qb[e][:, r.q0:r.q0 + r.m], kb[e][:, k0:k0 + n], start=False, stop=not last)
                        if last:
                            mm = pe.matmul(sps[k % S_RING][0:r.m, r.mask0:r.mask0 + r.m], keep["identb"][0:r.m, 0:r.m],
                                           keep["mask"][0:r.m, 0:r.m], start=False, stop=True)
                        mm.then_inc(s_full, 1)
                    elif ev[0] == "turn":
                        g = ev[1]
                        u = g["unit"]
                        pe.wait_ge(exp_ok, NS * j + u["score1"] + S_RING)
                        pe.wait_ge(lo_ok, ring(g["turn"], T_RING, NT, j))
                        bank = pps[g["turn"] % T_RING]
                        src = w[u["n"] % P_RING]
                        k = 2 * g["g"]
                        if u["rows"][0].dec:
                            pe.transpose(bank[:, 0:P], src[0][:, 0:P], keep["ident"][:, :])
                            mm = pe.transpose(bank[:, P:2 * P], src[0][:, DEC:DEC + PAST], keep["ident"][:, :])
                        else:
                            blocks = [(0, k), (1, k), (1, k + 1)] if g["last"] else [(0, k), (1, k), (0, k + 1), (1, k + 1)]
                            for n, (q, kt) in enumerate(blocks):
                                mm = pe.transpose(bank[:, n * P:(n + 1) * P], src[q][:, kt * P:(kt + 1) * P], keep["ident"][:, :])
                        mm.then_inc(turned, 1)
                    elif ev[0] == "value":
                        g = ev[1]
                        u = g["unit"]
                        e = u["head"]
                        if g["g"] == 0:
                            pe.wait_ge(out_ok, ring(u["n"], O_RING, NU, j))
                        pe.wait_ge(lo_ok, NT * j + g["turn"] + 1 + T_RING)
                        bank = ops[u["n"] % O_RING]
                        k = 2 * g["g"]
                        if u["rows"][0].dec:
                            uses = [(NQ, DEC, 0, DEC, 0), (NQ + 1, P, P, DEC, 0)]
                        elif g["last"]:
                            uses = [(k, P, 0, 256, 0), (k + 1, P, 256, P, P)]
                        else:
                            uses = [(k, P, 0, 256, 0), (k + 1, P, 256, 256, 0)]
                        for i, (kt, rows, c0, n, o0) in enumerate(uses):
                            for part in (whi, wlo):
                                mm = pe.matmul(bank[:, o0:o0 + n], vt[e][0:rows, kt, :], part[g["real"] % W_RING][0:rows, c0:c0 + n],
                                               start=(g["g"] == 0 and i == 0 and part is whi),
                                               stop=(g["last"] and i == 1 and part is wlo))
                        mm.then_inc(val_ok, 1)
                    elif ev[0] == "den":
                        _, e, turn = ev
                        pe.wait_ge(den_ok, 4 * j + 2 * e + 2)
                        pe.wait_ge(lo_ok, ring(turn, T_RING, NT, j))
                        pe.transpose(pps[turn % T_RING][0:RH, 0:P], den[:, e, 1, :], keep["ident"][:, :]).then_inc(turned, 1)

        @block.scalar
        def _(act):
            act.wait_ge(ready, 1)
            with act.Fori(0, PAIRS) as j:
                for ev in plan.events:
                    if ev[0] == "score" and ev[3] == len(ev[2].chunks) - 1:
                        r = ev[2]
                        u = r.unit
                        act.wait_ge(mx, NR * j + r.n + 1)
                        act.wait_ge(turned, 1 + NT * j + (plan.units[u["n"] - P_RING]["turn_end"] if u["n"] >= P_RING else 0))
                        first = ev[1] - len(r.chunks) + 1
                        at = 4 if len(r.chunks) > 1 else 0
                        for c, (_, n) in enumerate(r.chunks):
                            act.activation(w[u["n"] % P_RING][r.slot][0:r.m, c * 512:c * 512 + n],
                                           sps[(first + c) % S_RING][0:r.m, 0:n], ACT.Exp, bias=nmax[0:r.m, r.n, at:at + 1],
                                           accum_out=lsum[0:r.m, r.n, c:c + 1]).then_inc(exp_ok, 1)
                    elif ev[0] == "turn":
                        g = ev[1]
                        act.wait_ge(turned, 1 + NT * j + g["turn"] + 1)
                        act.wait_ge(val_ok, ring(g["real"], W_RING, NG, j))
                        for rows, c0, c1 in pieces(g):
                            last = act.activation(whi[g["real"] % W_RING][0:rows, c0:c1], pps[g["turn"] % T_RING][0:rows, c0:c1], ACT.Copy)
                        last.then_inc(hi_ok, 1)
                    elif ev[0] == "out":
                        u = ev[1]
                        n, b = u["n"], u["n"] % O_RING
                        act.wait_ge(val_ok, NG * j + u["groups"][-1]["real"] + 1 + W_RING)
                        act.wait_ge(out_ok, ring(n, O_RING, NU, j))
                        main, low = halves(u["head"])
                        cols = DEC if u["rows"][0].dec else 256
                        act.activation(tmp[main, b, 0:cols], ops[b][low, 0:cols], ACT.Copy).then_inc(low_out, 1)

        @block.vector
        def _(dve):
            dve.wait_ge(ready, 1)
            with dve.Fori(0, PAIRS) as j:
                parts = 0
                for ev in plan.events:
                    if ev[0] == "score":
                        _, k, r, c = ev
                        n = r.chunks[c][1]
                        dve.wait_ge(s_full, NS * j + k + 1)
                        red = dve.tensor_reduce(nmax[0:r.m, r.n, c:c + 1], sps[k % S_RING][0:r.m, 0:n], AX, ALU.max, negate=True)
                        if len(r.chunks) == 1:
                            red.then_inc(mx, 1)
                        else:
                            red.then_inc(mx_part, 1)
                            if c == len(r.chunks) - 1:
                                dve.wait_ge(mx_part, NM * j + r.max_end)
                                dve.tensor_reduce(nmax[:, r.n, 4:5], nmax[:, r.n, 0:c + 1], AX, ALU.min).then_inc(mx, 1)
                    elif ev[0] == "turn":
                        g = ev[1]
                        dve.wait_ge(hi_ok, NG * j + g["real"] + 1)
                        b = g["real"] % W_RING
                        for rows, c0, c1 in pieces(g):
                            last = dve.tensor_tensor(wlo[b][0:rows, c0:c1], pps[g["turn"] % T_RING][0:rows, c0:c1],
                                                     raw(whi[b][0:rows, c0:c1]), ALU.subtract)
                        last.then_inc(lo_ok, 1)
                    elif ev[0] == "out":
                        u = ev[1]
                        n, b, e = u["n"], u["n"] % O_RING, u["head"]
                        dve.wait_ge(low_out, NU * j + n + 1)
                        if n % (NU // 2) == 0:
                            dve.wait_ge(zstep, Z0 + 4 * NCH * (2 * j + e) - 4 * NCH)
                        main, _ = halves(e)
                        cols = DEC if u["rows"][0].dec else 256
                        q0 = u["rows"][0].q0
                        dve.tensor_tensor(att[main, q0:q0 + cols], ops[b][main, 0:cols], tmp[main, b, 0:cols], ALU.add).then_inc(out_ok, 1)
                    elif ev[0] == "den":
                        _, e, turn = ev
                        dve.wait_ge(exp_ok, NS * j + plan.units[(e + 1) * NU // 2 - 1]["score1"] + S_RING)
                        dve.tensor_reduce(den[:, e, 0, :], lsum[:, e * RH:(e + 1) * RH, :], AX, ALU.add).then_inc(den_ok, 1)
                        dve.wait_ge(den_ok, 4 * j + 2 * e + 1)
                        dve.reciprocal(den[:, e, 1, :], den[:, e, 0, :]).then_inc(den_ok, 1)
                        dve.wait_ge(turned, 1 + NT * j + turn + 1)
                        dve.wait_ge(zstep, Z0 + 4 * NCH * (2 * j + e) - 4 * NCH)
                        dve.tensor_copy(rdt[:, e, :], pps[turn % T_RING][0:RH, 0:P]).then_inc(lo_ok, 1)

        @block.gpsimd
        def _(pool):
            pool.memset(zeros[:, :], 0.0).then_inc(zstep, 1)
            pool.memset(lsum[:, :, :], 0.0).then_inc(zstep, 1)
            pool.wait_ge(zstep, 2)
            for e in range(2):
                pool.memset(lsum[:, e * RH + RH - 1, 0:1], 1.0).then_inc(zstep, 1)
            pool.wait_ge(zstep, 4)
            for n, (sem, size) in enumerate(((exp_ok, S_RING), (lo_ok, T_RING), (val_ok, W_RING), (out_ok, O_RING),
                                             (turned, 1), (zstep, Z0 - 4), (zout, 16))):
                pool.memset(start[:, n:n + 1], 0.0).then_inc(sem, size)
            pool.memset(start[:, 7:8], 0.0).then_inc(ready, 1)
            with pool.Fori(0, PAIRS) as j:
                for e in range(2):
                    rows, _ = halves(e)
                    h = 2 * j + e
                    for c, (c0, n) in enumerate(CHUNKS):
                        base = Z0 + 4 * NCH * h + 4 * c
                        pool.wait_ge(zin, (32 + 32 * NCH) * h + 32 + 32 * (c + 1))
                        pool.tensor_tensor(zc[rows, 2, 0:n], zc[rows, 0, 0:n], zc[rows, 1, 0:n], ALU.mult).then_inc(zstep, 1)
                        pool.wait_ge(zstep, base + 1)
                        if c == 0:
                            pool.wait_ge(out_ok, NU * j + (NU // 2) * (e + 1) + O_RING)
                        pool.tensor_tensor(zc[rows, 2, 0:n], zc[rows, 2, 0:n], att[rows, c0:c0 + n], ALU.mult).then_inc(zstep, 1)
                        pool.wait_ge(zstep, base + 2)
                        pool.wait_ge(zout, 32 * NCH * h + 32 * c + 16)
                        pool.tensor_tensor(zhi[rows, 0:n], zc[rows, 2, 0:n], zeros[rows, 0:n], ALU.add).then_inc(zstep, 1)
                        pool.wait_ge(zstep, base + 3)
                        pool.tensor_tensor(zlo[rows, 0:n], zc[rows, 2, 0:n], raw(zhi[rows, 0:n]), ALU.subtract).then_inc(zstep, 1)


def stage_out(nc, io, keep, dram):
    NT = NQ + 1
    with Scope(nc, "fin") as s:
        wraw = s.sb("wraw", [P, 2, D])
        whi = s.sb("whi", [P, KT, D], F32R)
        wlo = s.sb("wlo", [P, KT, D], F32R)
        zh = [s.sb(f"zh{n}", [P, KT, P], F32R) for n in range(2)]
        zl = [s.sb(f"zl{n}", [P, KT, P], F32R) for n in range(2)]
        x = s.sb("x", [P, 2, D])
        y = s.sb("y", [P, 2, D])
        o = s.sb("o", [P, 2, D])
        gate = s.sb("gate", [P, 2, D])
        pick = s.sb("pick", [2, 2, P])
        frow = s.sb("frow", [1, D])
        fg = s.sb("fg", [P, D])
        st = s.sb("st", [P, 6, NT])
        acc = [s.ps(f"acc{n}", [P, D]) for n in range(2)]
        gps = s.ps("gps", [P, D])
        w_in = [s.sem(f"w_in{n}") for n in range(2)]
        w_hi, w_lo, f_in, pick_ok, gturn, g_ok = (s.sem(n) for n in ("w_hi", "w_lo", "f_in", "pick_ok", "gturn", "g_ok"))
        z_in = [s.sem(f"z_in{n}") for n in range(2)]
        x_in = [s.sem(f"x_in{n}") for n in range(2)]
        y_out = [s.sem(f"y_out{n}") for n in range(2)]
        full, yg, yr, sq, var, rs, nr, o_ok = (s.sem(n) for n in ("full", "yg", "yr", "sq", "var", "rs", "nr", "o_ok"))
        block = s.enter_context(nc.Block())
        wv = io["w_out"][0].rearrange("(k p) n -> p k n", p=P)
        W = [P] * NQ + [DEC]

        def store(act, t):
            n = W[t]
            act.wait_ge(o_ok, t + 1)
            dst = io["y_prompt"][0, t * P:t * P + n, :] if t < NQ else io["y_sample"][0]
            act.dma_start(dst, o[0:n, t % 2, :]).then_inc(y_out[t % 2], 16)

        @block.sync
        def _(sp):
            for t, n in enumerate(W):
                b = t % 2
                if t >= 2:
                    sp.wait_ge(full, t - 1)
                c0 = t * P
                sp.dma_start(raw(zh[b][:, :, 0:n]), dram["z"][0, :, :, c0:c0 + n].rearrange("k p c -> p k c")).then_inc(z_in[b], 16)
                sp.dma_start(raw(zl[b][:, :, 0:n]), dram["z"][1, :, :, c0:c0 + n].rearrange("k p c -> p k c")).then_inc(z_in[b], 16)
                if t >= 2:
                    sp.wait_ge(yr, 2 * (t - 1))
                sp.dma_start(x[0:n, b, :], io["x_prompt"][0, c0:c0 + n, :] if t < NQ else io["x_sample"][0]).then_inc(x_in[b], 16)

        @block.gpsimd
        def _(pool):
            pool.dma_start(frow[:, :], io["final_g"].rearrange("(a d) -> a d", a=1)).then_inc(f_in, 16)
            pool.memset(pick[:, :, :], 1.0).then_inc(pick_ok, 1)
            pool.wait_ge(pick_ok, 1)
            pool.affine_select(out=pick[:, :, :], in_=pick[:, :, :], compare_op=ALU.is_equal, fill=0.0, base=0,
                               pattern=[[-1, 2], [0, P]], channel_multiplier=1).then_inc(pick_ok, 1)

        @block.tensor
        def _(pe):
            pe.wait_ge(pick_ok, 2)
            for which in range(2):
                if which:
                    pe.wait_ge(g_ok, which)
                for n in range(2):
                    mm = pe.matmul(gps[:, n * 512:(n + 1) * 512], pick[:, which, :], keep["gate"][:, n * 512:(n + 1) * 512],
                                   start=True, stop=True)
                mm.then_inc(gturn, 1)
            pe.wait_ge(g_ok, 2)
            pe.wait_ge(f_in, 16)
            for n in range(2):
                mm = pe.matmul(gps[:, n * 512:(n + 1) * 512], pick[0:1, 0, :], frow[:, n * 512:(n + 1) * 512], start=True, stop=True)
            mm.then_inc(gturn, 1)
            for t, n in enumerate(W):
                b = t % 2
                pe.wait_ge(z_in[b], 32 * (t // 2 + 1))
                if t >= 2:
                    pe.wait_ge(yg, 2 * (t - 1))
                for k in range(KT):
                    if t == 0:
                        pe.wait_ge(w_lo, k + 1)
                    for m in range(2):
                        cols = slice(m * 512, (m + 1) * 512)
                        out = acc[b][0:n, cols]
                        pe.matmul(out, zh[b][:, k, 0:n], whi[:, k, cols], start=(k == 0), stop=False)
                        pe.matmul(out, zh[b][:, k, 0:n], wlo[:, k, cols], start=False, stop=False)
                        mm = pe.matmul(out, zl[b][:, k, 0:n], whi[:, k, cols], start=False, stop=(k == KT - 1))
                mm.then_inc(full, 1)

        @block.scalar
        def _(act):
            for k in range(KT):
                if k >= 2:
                    act.wait_ge(w_lo, k - 1)
                act.dma_start(wraw[:, k % 2, :], wv[:, k, :]).then_inc(w_in[k % 2], 16)
                act.wait_ge(w_in[k % 2], 16 * (k // 2 + 1))
                act.activation(whi[:, k, :], wraw[:, k % 2, :], ACT.Copy).then_inc(w_hi, 1)
            for n in range(3):
                act.wait_ge(gturn, n + 1)
                act.activation(fg[:, :] if n == 2 else gate[:, n, :], gps[:, :], ACT.Copy).then_inc(g_ok, 1)
            for t, n in enumerate(W):
                b = t % 2
                act.wait_ge(yr, 2 * (t + 1))
                if t >= 2:
                    act.wait_ge(y_out[b], 16 * (t // 2))
                act.activation(o[0:n, b, :], y[0:n, b, :], ACT.Square, accum_out=st[0:n, 0, t:t + 1]).then_inc(sq, 1)
                act.wait_ge(var, 2 * t + 2)
                act.activation(st[0:n, 3, t:t + 1], st[0:n, 2, t:t + 1], ACT.Sqrt).then_inc(rs, 1)
                if t >= 1:
                    store(act, t - 1)
            store(act, NT - 1)
            for n in range(2):
                act.wait_ge(y_out[n], 16 * len(W[n::2]))

        @block.vector
        def _(dve):
            for k in range(KT):
                dve.wait_ge(w_hi, k + 1)
                dve.tensor_tensor(wlo[:, k, :], wraw[:, k % 2, :], raw(whi[:, k, :]), ALU.subtract).then_inc(w_lo, 1)

            def finish(t):
                n = W[t]
                r = [st[0:n, i, t:t + 1] for i in range(6)]
                dve.wait_ge(sq, t + 1)
                dve.tensor_scalar(r[1], r[0], 1.0 / D, EPS, ALU.mult, ALU.add).then_inc(var, 1)
                dve.wait_ge(var, 2 * t + 1)
                dve.reciprocal(r[2], r[1]).then_inc(var, 1)
                dve.wait_ge(rs, t + 1)
                dve.tensor_scalar(r[4], r[3], r[3], r[1], ALU.mult, ALU.mult).then_inc(nr, 1)
                dve.wait_ge(nr, 3 * t + 1)
                dve.tensor_scalar(r[5], r[4], -0.5, 1.5, ALU.mult, ALU.add).then_inc(nr, 1)
                dve.wait_ge(nr, 3 * t + 2)
                dve.tensor_scalar(r[4], r[5], r[3], None, ALU.mult).then_inc(nr, 1)
                dve.wait_ge(nr, 3 * t + 3)
                dve.scalar_tensor_tensor(out=o[0:n, t % 2, :], in0=y[0:n, t % 2, :], scalar=r[4], in1=fg[0:n, :],
                                         op0=ALU.mult, op1=ALU.mult).then_inc(o_ok, 1)

            dve.wait_ge(g_ok, 3)
            for t, n in enumerate(W):
                b = t % 2
                which = 0 if t < NQ else 1
                dve.wait_ge(full, t + 1)
                if t >= 2:
                    dve.wait_ge(o_ok, t - 1)
                for m in range(2):
                    cols = slice(m * 512, (m + 1) * 512)
                    dve.tensor_tensor(y[0:n, b, cols], acc[b][0:n, cols], gate[0:n, which, cols], ALU.mult).then_inc(yg, 1)
                dve.wait_ge(x_in[b], 16 * (t // 2 + 1))
                for m in range(2):
                    cols = slice(m * 512, (m + 1) * 512)
                    dve.wait_ge(yg, 2 * t + m + 1)
                    dve.tensor_tensor(y[0:n, b, cols], y[0:n, b, cols], x[0:n, b, cols], ALU.add).then_inc(yr, 1)
                if t >= 1:
                    finish(t - 1)
            finish(NT - 1)


_IN = ["x_prompt", "x_sample", "c_prompt", "c_sample", "cache_k", "cache_v", "cache_logf", "state_pool",
       "norm_g", "w_ada", "b_ada", "w_in", "b_f", "w_pool", "pool_scale", "w_out", "final_g"]
_OUT = [("y_prompt", (1, SEQ, D)), ("y_sample", (1, DEC, D)),
        ("k_prompt", (1, 1, SEQ, HEADS, DH)), ("v_prompt", (1, 1, SEQ, HEADS, DH)), ("logf_prompt", (1, 1, SEQ, HEADS)),
        ("pool_prompt", (1, 1, HIST, A)),
        ("k_sample", (1, 1, DEC, HEADS, DH)), ("v_sample", (1, 1, DEC, HEADS, DH)), ("logf_sample", (1, 1, DEC, HEADS)),
        ("pool_sample", (1, 1, HIST, A))]
_SCRATCH = {"v": [NQ + 2, P, HEADS * P], "k": [PAIRS, 2, P, TC], "q": [PAIRS, 2, P, T], "kf": [PAIRS, P, T],
            "u": [GROUPS, P, T], "pg": [GROUPS, P, T], "ag": [PAIRS, P, T], "d": [2, GROUPS, P, T],
            "fq": [HEADS, 4, TC], "fk": [HEADS, 4, TC], "z": [2, KT, P, T], "rden": [HEADS, T]}


def build(nc, io):
    dram = {n: nc.dram_tensor(f"scratch_{n}", s, F32, kind="Internal").ap() for n, s in _SCRATCH.items()}
    with Scope(nc, "keep") as s:
        keep = {
            "ident": s.sb("ident", [P, P]), "identb": s.sb("identb", [P, P], BF16), "mask": s.sb("mask", [P, P], BF16),
            "cols": s.sb("cols", [P, NROWS]), "bf": s.sb("bf", [HEADS, 1]), "gate": s.sb("gate", [2, D]),
            "shift": s.sb("shift", [P, KT, 2]), "scale": s.sb("scale", [P, KT, 2]),
        }
        stage_ada(nc, io, keep)
        stage_project(nc, io, keep, dram)
        stage_pool(nc, io, keep, dram)
        stage_attend(nc, io, keep, dram)
        stage_out(nc, io, keep, dram)


def kernel(**inputs):
    import concourse.bacc as bacc
    import numpy as np
    from concourse.bass_utils import run_bass_kernel_spmd

    nc = bacc.Bacc("TRN2", target_bir_lowering=False, num_devices=1)
    arrays, io = {}, {}
    for name in _IN:
        a = np.ascontiguousarray(inputs[name])
        arrays[f"in_{name}"] = a
        io[name] = nc.dram_tensor(f"in_{name}", a.shape, mybir.dt.from_np(a.dtype), kind="ExternalInput").ap()
    for name, shape in _OUT:
        io[name] = nc.dram_tensor(f"out_{name}", shape, F32, kind="ExternalOutput").ap()
    build(nc, io)
    r = run_bass_kernel_spmd(nc, [arrays], core_ids=[0])
    return tuple(r.results[0][f"out_{name}"] for name, _ in _OUT)
```

```python
from contextlib import ExitStack

import concourse.bass as bass
from concourse import mybir

F32 = mybir.dt.float32
F32R = mybir.dt.float32r
BF16 = mybir.dt.bfloat16
ALU = mybir.AluOpType
ACT = mybir.ActivationFunctionType
AX = mybir.AxisListType.X

P = 128
D = 1024
KT = D // P
SEQ = 2048
DEC = 64
PAST = 128
HEADS = 8
DH = 64
PAIRS = HEADS // 2
GROUPS = 4
WINDOWS = (2, 4, 8, 16)
HIST = 15
A = 512
T = SEQ + DEC
TC = T + PAST
NQ = SEQ // P
EPS = 1e-6
SCALE = 1.0 / 8.0
MASKED = -1e30
CHUNKS = [(0, 512), (512, 512), (1024, 512), (1536, 288), (1824, 288)]
NCH = len(CHUNKS)
COL_Q, COL_K, COL_V, COL_AG, COL_F = 0, A, 2 * A, 3 * A, 4 * A
COL_U = COL_F + HEADS
COL_PG = COL_U + A
ROW_CP, ROW_CS, ROW_G, ROW_B, ROW_PS, NROWS = 0, 8, 16, 24, 48, 52


class Scope(ExitStack):

    def __init__(self, nc, tag):
        super().__init__()
        self.nc, self.tag = nc, tag

    def sb(self, name, shape, dt=F32):
        return self.enter_context(self.nc.sbuf_tensor(f"{self.tag}_{name}", shape, dt))

    def ps(self, name, shape, dt=F32):
        return self.enter_context(self.nc.psum_tensor(f"{self.tag}_{name}", shape, dt))

    def sem(self, name):
        return self.enter_context(self.nc.semaphore(f"{self.tag}_{name}"))


def raw(x):
    return x.bitcast(F32)


def stage_ada(nc, io, keep):
    with Scope(nc, "ada") as s:
        w = s.sb("w", [P, KT, 3 * D])
        rows = s.sb("rows", [NROWS, P])
        sc = s.sb("silu", [P, 2 * KT])
        mrow = s.sb("mrow", [2, 2 * D])
        one_b = s.sb("one_b", [P, 24])
        gate_b = s.sb("gate_b", [2, D])
        acc = [s.ps(f"acc{n}", [P, 512]) for n in range(6)]
        tps = s.ps("tps", [P, 512])
        cps = s.ps("cps", [P, 512])
        rows_in = s.sem("rows_in")
        w_in = [s.sem(f"w_in{k}") for k in range(KT // 2)]
        g_in = s.sem("g_in")
        gb_in = s.sem("gb_in")
        const = s.sem("const")
        turned = s.sem("turned")
        cols_ok = s.sem("cols_ok")
        silu_ok = s.sem("silu_ok")
        m_full = s.sem("m_full")
        m_row = s.sem("m_row")
        m_col = s.sem("m_col")
        ab = s.sem("ab")
        cols, ident = keep["cols"], keep["ident"]
        wv = io["w_ada"][0].rearrange("(k p) n -> p k n", p=P)
        block = s.enter_context(nc.Block())

        @block.sync
        def _(sp):
            small = [("c_prompt", ROW_CP, KT), ("c_sample", ROW_CS, KT), ("norm_g", ROW_G, KT),
                     ("b_ada", ROW_B, 24), ("pool_scale", ROW_PS, GROUPS)]
            for name, r, n in small:
                sp.dma_start(rows[r:r + n, :], io[name].rearrange("a (k p) -> (a k) p", p=P)).then_inc(rows_in, 16)
            sp.dma_start(keep["bf"][:, :], io["b_f"].rearrange("a h -> h a")).then_inc(rows_in, 16)
            for k in range(0, KT, 2):
                sp.dma_start(w[:, k:k + 2, 0:2 * D], wv[:, k:k + 2, 0:2 * D]).then_inc(w_in[k // 2], 16)
            sp.dma_start(w[:, :, 2 * D:], wv[:, :, 2 * D:]).then_inc(g_in, 16)
            sp.dma_start(gate_b[:, :], io["b_ada"][:, 2 * D:].partition_broadcast(2)).then_inc(gb_in, 16)

        @block.scalar
        def _(act):
            act.wait_ge(cols_ok, 1)
            act.activation(sc[:, :], cols[:, ROW_CP:ROW_CP + 2 * KT], ACT.Silu).then_inc(silu_ok, 1)
            act.wait_ge(m_full, 1)
            for n in range(4):
                act.activation(mrow[:, n * 512:(n + 1) * 512], acc[n][0:2, :], ACT.Copy).then_inc(m_row, 1)
            act.wait_ge(rows_in, 96)
            act.wait_ge(m_row, 4)

        @block.gpsimd
        def _(pool):
            pool.memset(ident[:, :], 0.0).then_inc(const, 1)
            pool.memset(keep["mask"][:, :], 0.0).then_inc(const, 1)
            pool.wait_ge(const, 2)
            pool.affine_select(out=ident[:, :], in_=ident[:, :], compare_op=ALU.not_equal, fill=1.0, base=0,
                               pattern=[[-1, P]], channel_multiplier=1).then_inc(const, 1)
            pool.affine_select(out=keep["mask"][:, :], in_=keep["mask"][:, :], compare_op=ALU.is_ge, fill=MASKED,
                               base=0, pattern=[[-1, P]], channel_multiplier=1).then_inc(const, 1)
            pool.wait_ge(const, 4)
            pool.tensor_copy(keep["identb"][:, :], ident[:, :]).then_inc(const, 1)
            pool.wait_ge(const, 5)

        @block.tensor
        def _(pe):
            pe.wait_ge(rows_in, 96)
            pe.wait_ge(const, 3)
            pe.transpose(tps[:, 0:NROWS], rows[:, :], ident[0:NROWS, 0:NROWS]).then_inc(turned, 1)
            pe.wait_ge(silu_ok, 1)
            pair = sc[:, :].rearrange("p (w k) -> p k w", w=2)
            for k in range(KT):
                pe.wait_ge(w_in[k // 2], 16)
                for n in range(4):
                    mm = pe.matmul(acc[n][0:2, :], pair[:, k, :], w[:, k, n * 512:(n + 1) * 512],
                                   start=(k == 0), stop=(k == KT - 1))
            mm.then_inc(m_full, 1)
            pe.wait_ge(m_row, 4)
            for n in range(2 * KT):
                mm = pe.transpose(cps[:, 2 * n:2 * n + 2], mrow[:, n * P:(n + 1) * P], ident[0:2, 0:2])
            mm.then_inc(m_col, 1)
            pe.wait_ge(g_in, 16)
            for k in range(KT):
                for n in range(2):
                    mm = pe.matmul(acc[4 + n][0:2, :], pair[:, k, :], w[:, k, 2 * D + n * 512:2 * D + (n + 1) * 512],
                                   start=(k == 0), stop=(k == KT - 1))
            mm.then_inc(m_full, 1)

        @block.vector
        def _(dve):
            dve.wait_ge(turned, 1)
            dve.tensor_copy(cols[:, :], tps[:, 0:NROWS]).then_inc(cols_ok, 1)
            dve.wait_ge(cols_ok, 1)
            dve.tensor_scalar(one_b[:, :], cols[:, ROW_B:ROW_B + 24], 1.0, None, ALU.add).then_inc(ab, 1)
            dve.wait_ge(m_col, 1)
            dve.wait_ge(ab, 1)
            for k in range(KT):
                dve.tensor_scalar(keep["shift"][:, k, :], cps[:, 2 * k:2 * k + 2],
                                  cols[:, ROW_B + k:ROW_B + k + 1], None, ALU.add).then_inc(ab, 1)
                dve.tensor_scalar(keep["scale"][:, k, :], cps[:, 2 * (KT + k):2 * (KT + k) + 2],
                                  one_b[:, KT + k:KT + k + 1], cols[:, ROW_G + k:ROW_G + k + 1],
                                  ALU.add, ALU.mult).then_inc(ab, 1)
            dve.wait_ge(m_full, 2)
            dve.wait_ge(gb_in, 16)
            for n in range(2):
                cs = slice(n * 512, (n + 1) * 512)
                dve.tensor_tensor(keep["gate"][:, cs], acc[4 + n][0:2, :], gate_b[:, cs], ALU.add).then_inc(ab, 1)
            dve.wait_ge(ab, 1 + 2 * KT + 2)


def stage_project(nc, io, keep, dram):
    with Scope(nc, "prj") as s:
        hhi = s.sb("hhi", [P, KT, T], F32R)
        hlo = s.sb("hlo", [P, KT, T], F32R)
        sv = Scope(nc, "prv")
        stage_values(nc, io, keep, dram, hhi, hlo, sv)
        stage_tiles(nc, io, keep, dram, hhi, hlo)


def stage_values(nc, io, keep, dram, hhi, hlo, s):
    NT = SEQ // P + 1
    with s:
        vhi_w = s.sb("vhi_w", [P, KT, 512], F32R)
        vlo_w = s.sb("vlo_w", [P, KT, 512], F32R)
        xt = s.sb("xt", [P, 2, D])
        xn = s.sb("xn", [P, D])
        junk = s.sb("junk", [P, D], BF16)
        hf = s.sb("hf", [P, 2, D])
        vf = s.sb("vf", [P, 2, 512])
        vs = s.sb("vs", [P, 2, HEADS, P], F32R)
        wraw = raw(vs[:, :, :, :]).rearrange("p b h c -> p (b h c)").rearrange("p (b c) -> p b c", b=4)
        st = s.sb("st", [P, 6, NT])
        xps = [s.ps(f"xps{n}", [P, D]) for n in range(2)]
        vps = [s.ps(f"vps{n}", [P, 512]) for n in range(2)]
        wr_in = [s.sem(f"wr_in{n}") for n in range(4)]
        w_hi, w_lo = s.sem("w_hi"), s.sem("w_lo")
        x_in = [s.sem(f"x_in{n}") for n in range(2)]
        sq, var, rs, nr, xn_ok = s.sem("sq"), s.sem("var"), s.sem("rs"), s.sem("nr"), s.sem("xn_ok")
        xturn, hf_ok, hi_ok, lo_ok = s.sem("xturn"), s.sem("hf_ok"), s.sem("hi_ok"), s.sem("lo_ok")
        v_full, vf_ok, vhi_ok, vlo_ok = s.sem("v_full"), s.sem("vf_ok"), s.sem("vhi_ok"), s.sem("vlo_ok")
        v_out = [s.sem(f"v_out{n}") for n in range(2)]
        vs_out = [s.sem(f"vs_out{n}") for n in range(2)]
        cv_in = s.sem("cv_in")
        block = s.enter_context(nc.Block())
        wv = io["w_in"][0].rearrange("(k p) n -> p k n", p=P)

        def rows_of(t):
            return P if t < NT - 1 else DEC

        def x_of(t):
            return io["x_prompt"][0, t * P:(t + 1) * P, :] if t < NT - 1 else io["x_sample"][0]

        def split_slots(t, even):
            v = vs[:, t % 2, :, :].rearrange("p (g e) c -> p g e c", e=2)
            return (v[:, :, 0, 0:DH], v[:, :, 1, DH:P]) if even else (v[:, :, 0, DH:P], v[:, :, 1, 0:DH])

        def heads(x):
            v = x.rearrange("p (g e d) -> p g e d", e=2, d=DH)
            return v[:, :, 0, :], v[:, :, 1, :]

        def store(sp, t):
            n = rows_of(t)
            sp.wait_ge(vf_ok, t + 1)
            dst = io["v_prompt"][0, 0, t * P:(t + 1) * P] if t < NT - 1 else io["v_sample"][0, 0]
            sp.dma_start(dst.rearrange("s h d -> s (h d)"), vf[0:n, t % 2, :]).then_inc(v_out[t % 2], 16)
            sp.wait_ge(vlo_ok, t + 1)
            sp.dma_start(dram["v"][t, 0:n, :], raw(vs[0:n, t % 2, :, :]).rearrange("p h c -> p (h c)")).then_inc(vs_out[t % 2], 16)

        def values(act, t, src, n, full):
            if full:
                act.wait_ge(v_full, t + 1)
                if t >= 2:
                    act.wait_ge(v_out[t % 2], 16 * (t // 2))
                act.activation(vf[0:n, t % 2, :], src, ACT.Copy).then_inc(vf_ok, 1)
            if t >= 2:
                act.wait_ge(vs_out[t % 2], 16 * (t // 2))
            for d, x in zip(split_slots(t, True), heads(src)):
                last = act.activation(d[0:n], x, ACT.Copy)
            last.then_inc(vhi_ok, 1)

        def lows(dve, t, src, n):
            dve.wait_ge(vhi_ok, t + 1)
            for d, x, hi in zip(split_slots(t, False), heads(src), split_slots(t, True)):
                last = dve.tensor_tensor(d[0:n], x, raw(hi[0:n]), ALU.subtract)
            last.then_inc(vlo_ok, 1)

        @block.sync
        def _(sp):
            for t in range(NT):
                store(sp, t)
            b = NT % 2
            sp.wait_ge(vlo_ok, NT - 1)
            sp.wait_ge(v_out[b], 16 * (NT // 2))
            sp.dma_start(vf[:, b, :], io["cache_v"][0, 0].rearrange("s h d -> s (h d)")).then_inc(cv_in, 16)
            sp.wait_ge(vhi_ok, NT + 1)
            sp.wait_ge(vlo_ok, NT + 1)
            sp.dma_start(dram["v"][NT, :, :], raw(vs[:, b, :, :]).rearrange("p h c -> p (h c)")).then_inc(vs_out[b], 16)
            for n in range(2):
                sp.wait_ge(v_out[n], 16 * len(range(n, NT, 2)))
                sp.wait_ge(vs_out[n], 16 * len(range(n, NT + 1, 2)))

        @block.scalar
        def _(act):
            def load_x(t):
                if t >= NT:
                    return
                n = rows_of(t)
                if t >= 2:
                    act.wait_ge(xn_ok, t - 1)
                act.dma_start(xt[0:n, t % 2, :], x_of(t)).then_inc(x_in[t % 2], 16)

            load_x(0)
            load_x(1)
            for k in range(KT):
                if k >= 4:
                    act.wait_ge(w_lo, k - 3)
                act.dma_start(wraw[:, k % 4, :], wv[:, k, COL_V:COL_V + A]).then_inc(wr_in[k % 4], 16)

            def square(t):
                n = rows_of(t)
                act.wait_ge(x_in[t % 2], 16 * (t // 2 + 1))
                if t >= 1:
                    act.wait_ge(sq, t)
                act.activation(junk[0:n, :], xt[0:n, t % 2, :], ACT.Square, accum_out=st[0:n, 0, t:t + 1]).then_inc(sq, 1)

            def root(t):
                n = rows_of(t)
                act.wait_ge(var, 2 * t + 2)
                act.activation(st[0:n, 3, t:t + 1], st[0:n, 2, t:t + 1], ACT.Sqrt).then_inc(rs, 1)

            def norm(t):
                n = rows_of(t)
                if t >= 1:
                    act.wait_ge(xturn, t)
                act.wait_ge(nr, 3 * t + 3)
                act.activation(xn[0:n, :], xt[0:n, t % 2, :], ACT.Copy, scale=st[0:n, 5, t:t + 1]).then_inc(xn_ok, 1)
                load_x(t + 2)

            def high(t):
                n = rows_of(t)
                act.wait_ge(hf_ok, KT * (t + 1))
                act.activation(hhi[:, :, t * P:t * P + n], hf[:, t % 2, :].rearrange("p (k c) -> p k c", k=KT)[:, :, 0:n],
                               ACT.Copy).then_inc(hi_ok, 1)

            for t in range(3):
                square(t)
                root(t)
                norm(t)
            square(3)
            root(3)
            high(0)
            for t in range(NT):
                if t + 3 < NT:
                    norm(t + 3)
                if t + 1 < NT:
                    high(t + 1)
                if t + 4 < NT:
                    square(t + 4)
                if t + 4 < NT:
                    root(t + 4)
                values(act, t, vps[t % 2][0:rows_of(t), :], rows_of(t), True)
            act.wait_ge(cv_in, 16)
            b = NT % 2
            values(act, NT, vf[:, b, :], P, False)

        @block.gpsimd
        def _(pool):
            for t in range(NT):
                n = rows_of(t)
                pool.wait_ge(hi_ok, t + 1)
                pool.tensor_tensor(hlo[:, :, t * P:t * P + n], hf[:, t % 2, :].rearrange("p (k c) -> p k c", k=KT)[:, :, 0:n],
                                   raw(hhi[:, :, t * P:t * P + n]), ALU.subtract).then_inc(lo_ok, 1)

        @block.vector
        def _(dve):
            for k in range(KT):
                dve.wait_ge(wr_in[k % 4], 16 * (k // 4 + 1))
                dve.tensor_copy(vhi_w[:, k, :], wraw[:, k % 4, :]).then_inc(w_hi, 1)
                dve.wait_ge(w_hi, k + 1)
                dve.tensor_tensor(vlo_w[:, k, :], wraw[:, k % 4, :], raw(vhi_w[:, k, :]), ALU.subtract).then_inc(w_lo, 1)

            def stats(t):
                n = rows_of(t)
                dve.wait_ge(sq, t + 1)
                dve.tensor_scalar(st[0:n, 1, t:t + 1], st[0:n, 0, t:t + 1], 1.0 / D, EPS, ALU.mult, ALU.add).then_inc(var, 1)
                dve.wait_ge(var, 2 * t + 1)
                dve.reciprocal(st[0:n, 2, t:t + 1], st[0:n, 1, t:t + 1]).then_inc(var, 1)
                dve.wait_ge(rs, t + 1)
                dve.tensor_scalar(st[0:n, 4, t:t + 1], st[0:n, 3, t:t + 1], st[0:n, 3, t:t + 1], st[0:n, 1, t:t + 1],
                                  ALU.mult, ALU.mult).then_inc(nr, 1)
                dve.wait_ge(nr, 3 * t + 1)
                dve.tensor_scalar(st[0:n, 5, t:t + 1], st[0:n, 4, t:t + 1], -0.5, 1.5, ALU.mult, ALU.add).then_inc(nr, 1)
                dve.wait_ge(nr, 3 * t + 2)
                dve.tensor_scalar(st[0:n, 5, t:t + 1], st[0:n, 5, t:t + 1], st[0:n, 3, t:t + 1], None, ALU.mult).then_inc(nr, 1)

            def modulate(t):
                n = rows_of(t)
                which = 0 if t < NT - 1 else 1
                dve.wait_ge(xturn, t + 1)
                if t >= 2:
                    dve.wait_ge(lo_ok, t - 1)
                for k in range(KT):
                    dve.tensor_scalar(hf[:, t % 2, k * P:k * P + n], xps[t % 2][:, k * P:k * P + n],
                                      keep["scale"][:, k, which:which + 1], keep["shift"][:, k, which:which + 1],
                                      ALU.mult, ALU.add).then_inc(hf_ok, 1)

            for t in range(3):
                stats(t)
            modulate(0)
            stats(3)
            modulate(1)
            for t in range(NT):
                if t + 4 < NT:
                    stats(t + 4)
                if t + 2 < NT:
                    modulate(t + 2)
                lows(dve, t, vps[t % 2][0:rows_of(t), :], rows_of(t))
            lows(dve, NT, vf[:, NT % 2, :], P)

        @block.tensor
        def _(pe):
            def turn(t):
                n = rows_of(t)
                pe.wait_ge(xn_ok, t + 1)
                if t >= 2:
                    pe.wait_ge(hf_ok, KT * (t - 1))
                for k in range(KT):
                    mm = pe.transpose(xps[t % 2][:, k * P:k * P + n], xn[0:n, k * P:(k + 1) * P], keep["ident"][0:n, 0:n])
                mm.then_inc(xturn, 1)

            turn(0)
            turn(1)
            for t in range(NT):
                n = rows_of(t)
                if t + 2 < NT:
                    turn(t + 2)
                pe.wait_ge(lo_ok, t + 1)
                if t >= 2:
                    pe.wait_ge(vlo_ok, t - 1)
                cols = slice(t * P, t * P + n)
                for k in range(KT):
                    if t == 0:
                        pe.wait_ge(w_lo, k + 1)
                    pe.matmul(vps[t % 2][0:n, :], hhi[:, k, cols], vhi_w[:, k, :], start=(k == 0), stop=False)
                    pe.matmul(vps[t % 2][0:n, :], hhi[:, k, cols], vlo_w[:, k, :], start=False, stop=False)
                    mm = pe.matmul(vps[t % 2][0:n, :], hlo[:, k, cols], vhi_w[:, k, :], start=False, stop=(k == KT - 1))
                mm.then_inc(v_full, 1)


def stage_forget(nc, io, keep, dram, hhi, hlo, acc, full, free, spt):
    NF = SEQ // P + 2
    ODD = [1.0 / n for n in (15, 13, 11, 9, 7, 5, 3)]
    with Scope(nc, "fgt") as s:
        wfr = s.sb("wfr", [P, KT, HEADS])
        wf = s.sb("wf", [P, KT, DH], F32R)
        low = s.sb("low", [HEADS, TC])
        fx = s.sb("fx", [HEADS, TC])
        lx = s.sb("lx", [P, 6, (NF - 1) * HEADS])
        lf = s.sb("lf", [P, NF, HEADS])
        lft = s.sb("lft", [HEADS, TC])
        ones = s.sb("ones", [HEADS, TC])
        run = s.sb("run", [HEADS, TC])
        hi_r = s.sb("hi_r", [HEADS, TC], F32R)
        run_lo, neg_hi, neg_lo = low, fx, lft
        ck = s.sb("ck", [P, A])
        ckhi = s.sb("ckhi", [P, A], F32R)
        cklo = s.sb("cklo", [P, A], F32R)
        sp_rows = s.sb("sp_rows", [HIST, A])
        tps = s.ps("tps", [P, 512])
        kps = s.ps("kps", [P, 512])
        hps = s.ps("hps", [P, 512])
        w_in, c_in = s.sem("w_in"), s.sem("c_in")
        w_ok = s.sem("w_ok")
        low_ok, fturn, lx_ok, ex, lf_ok = s.sem("low_ok"), s.sem("fturn"), s.sem("lx_ok"), s.sem("ex"), s.sem("lf_ok")
        bturn, lft_ok, one_ok, run_ok, part_ok = s.sem("bturn"), s.sem("lft_ok"), s.sem("one_ok"), s.sem("run_ok"), s.sem("part_ok")
        cturn, ckhi_ok, cklo_ok = s.sem("cturn"), s.sem("ckhi_ok"), s.sem("cklo_ok")
        out = s.sem("out")
        block = s.enter_context(nc.Block())
        ident = keep["ident"]
        wv = io["w_in"][0].rearrange("(k p) n -> p k n", p=P)
        NM = (NF - 1) * HEADS

        @block.sync
        def _(sp):
            sp.dma_start(wfr[:, :, :], wv[:, :, COL_F:COL_F + HEADS]).then_inc(w_in, 16)
            sp.dma_start(ck[:, :], io["cache_k"][0, 0].rearrange("s h d -> s (h d)")).then_inc(c_in, 16)
            sp.dma_start(sp_rows[:, :], io["state_pool"][0, 0]).then_inc(c_in, 16)
            sp.dma_start(lf[:, NF - 1, :], io["cache_logf"][0, 0]).then_inc(c_in, 16)
            sp.wait_ge(ckhi_ok, 1)
            sp.dma_start(dram["k"][:, 0, :, T:TC].rearrange("g p c -> p g c"),
                         raw(ckhi[:, :]).rearrange("p (g c) -> p g c", g=PAIRS)).then_inc(out, 16)
            sp.wait_ge(cklo_ok, 1)
            sp.dma_start(dram["k"][:, 1, :, T:TC].rearrange("g p c -> p g c"),
                         raw(cklo[:, :]).rearrange("p (g c) -> p g c", g=PAIRS)).then_inc(out, 16)
            sp.wait_ge(lf_ok, 1)
            sp.dma_start(io["logf_prompt"][0, 0].rearrange("(t p) h -> p t h", p=P), lf[:, 0:NQ, :]).then_inc(out, 16)
            sp.dma_start(io["logf_sample"][0, 0], lf[0:DEC, NQ, :]).then_inc(out, 16)
            sp.wait_ge(part_ok, 3)
            hi = raw(hi_r[:, :])
            for r, (q, k) in enumerate([(hi, ones), (ones, neg_hi), (run_lo, ones), (ones, neg_lo)]):
                sp.dma_start(dram["fq"][:, r, :], q[:, :]).then_inc(out, 16)
                sp.dma_start(dram["fk"][:, r, :], k[:, :]).then_inc(out, 16)
            sp.wait_ge(out, 16 * 12)

        @block.gpsimd
        def _(pool):
            pool.memset(raw(wf[:, :, :]), 0.0).then_inc(one_ok, 1)
            pool.memset(ones[:, :], 1.0).then_inc(one_ok, 1)

        @block.scalar
        def _(act):
            for c, (c0, n) in enumerate(CHUNKS):
                act.wait_ge(full, c + 1)
                act.activation(low[:, c0:c0 + n], acc[c][32:32 + HEADS, 0:n], ACT.Copy).then_inc(low_ok, 1)
            act.wait_ge(cturn, 1)
            act.activation(ckhi[:, :], kps[:, :], ACT.Copy).then_inc(ckhi_ok, 1)
            act.wait_ge(cturn, 2)
            act.activation(spt[:, :, :], hps[:, 0:GROUPS * 16].rearrange("p (g c) -> p g c", c=16)[:, :, 0:HIST],
                           ACT.Copy).then_inc(ckhi_ok, 1)
            act.wait_ge(lx_ok, 4)
            act.activation(lx[:, 2, :], lx[:, 1, :], ACT.Exp, scale=-1.0).then_inc(ex, 1)
            for b in range(NCH):
                n = 512 if b < 4 else DEC + PAST
                act.wait_ge(bturn, b + 1)
                act.activation(lft[:, b * 512:b * 512 + n], acc[b][0:HEADS, 0:n], ACT.Copy).then_inc(lft_ok, 1)
            act.wait_ge(lft_ok, NCH)
            act.wait_ge(ckhi_ok, 2)

        @block.tensor
        def _(pe):
            pe.wait_ge(w_ok, 2)
            for c, (c0, n) in enumerate(CHUNKS):
                for k in range(KT):
                    for h in (hhi, hlo):
                        mm = pe.matmul(acc[c][0:DH, 0:n], wf[:, k, :], h[:, k, c0:c0 + n],
                                       start=(k == 0 and h is hhi), stop=(k == KT - 1 and h is hlo))
                mm.then_inc(full, 1)
            pe.wait_ge(c_in, 48)
            for g in range(PAIRS):
                mm = pe.transpose(kps[:, g * P:(g + 1) * P], ck[:, g * P:(g + 1) * P], ident[:, :])
            mm.then_inc(cturn, 1)
            for g in range(GROUPS):
                mm = pe.transpose(hps[:, 16 * g:16 * g + HIST], sp_rows[:, g * P:(g + 1) * P], ident[0:HIST, 0:HIST])
            mm.then_inc(cturn, 1)
            pe.wait_ge(free, NCH)
            for t in range(NF - 1):
                n = min(P, T - t * P)
                mm = pe.transpose(tps[0:n, t * HEADS:(t + 1) * HEADS], fx[:, t * P:t * P + n], ident[0:HEADS, 0:HEADS])
            mm.then_inc(fturn, 1)
            pe.wait_ge(lf_ok, 1)
            for t in range(NF):
                n = DEC if t == NF - 2 else P
                b = min(t // 4, 4)
                c = t * P - b * 512 if t < NF - 1 else DEC
                mm = pe.transpose(acc[b][0:HEADS, c:c + n], lf[0:n, t, :], ident[0:n, 0:n])
                if t % 4 == 3 or t == NF - 1:
                    mm.then_inc(bturn, 1)

        @block.vector
        def _(dve):
            dve.wait_ge(w_in, 16)
            dve.wait_ge(one_ok, 1)
            dve.tensor_copy(wf[:, :, 0:HEADS], wfr[:, :, :]).then_inc(w_ok, 1)
            dve.wait_ge(w_ok, 1)
            dve.tensor_tensor(wf[:, :, 32:32 + HEADS], wfr[:, :, :], raw(wf[:, :, 0:HEADS]), ALU.subtract).then_inc(w_ok, 1)
            for c, (c0, n) in enumerate(CHUNKS):
                dve.wait_ge(low_ok, c + 1)
                dve.scalar_tensor_tensor(out=fx[:, c0:c0 + n], in0=acc[c][0:HEADS, 0:n], scalar=keep["bf"][:, 0:1],
                                         in1=low[:, c0:c0 + n], op0=ALU.add, op1=ALU.add).then_inc(free, 1)
            dve.wait_ge(ckhi_ok, 1)
            dve.tensor_tensor(cklo[:, :], kps[:, :], raw(ckhi[:, :]), ALU.subtract).then_inc(cklo_ok, 1)
            x, ax, e, sq, q, mn = (lx[:, i, :] for i in range(6))
            dve.memset(x, 0.0).then_inc(lx_ok, 1)
            dve.wait_ge(lx_ok, 1)
            dve.wait_ge(fturn, 1)
            dve.tensor_copy(lx[:, 0, 0:NQ * HEADS], tps[:, 0:NQ * HEADS]).then_inc(lx_ok, 1)
            dve.tensor_copy(lx[0:DEC, 0, NQ * HEADS:NM], tps[0:DEC, NQ * HEADS:NM]).then_inc(lx_ok, 1)
            dve.wait_ge(lx_ok, 3)
            dve.scalar_tensor_tensor(out=ax, in0=x, scalar=-1.0, in1=x, op0=ALU.mult, op1=ALU.max).then_inc(lx_ok, 1)
            dve.tensor_scalar(mn, x, 0.0, None, ALU.min).then_inc(lx_ok, 1)
            dve.wait_ge(ex, 1)
            count = 5

            def step(ins):
                nonlocal count
                count += 1
                ins.then_inc(lx_ok, 1)
                dve.wait_ge(lx_ok, count)

            step(dve.tensor_scalar(q, e, 2.0, None, ALU.add))
            step(dve.reciprocal(ax, q))
            step(dve.tensor_tensor(e, e, ax, ALU.mult))
            step(dve.tensor_tensor(sq, e, e, ALU.mult))
            step(dve.tensor_scalar(q, sq, 1.0 / 17, None, ALU.mult))
            for c in ODD:
                step(dve.scalar_tensor_tensor(out=q, in0=q, scalar=c, in1=sq, op0=ALU.add, op1=ALU.mult))
            step(dve.scalar_tensor_tensor(out=q, in0=q, scalar=1.0, in1=e, op0=ALU.add, op1=ALU.mult))
            dve.scalar_tensor_tensor(out=lf[:, 0:NF - 1, :], in0=q.rearrange("p (t h) -> p t h", h=HEADS), scalar=-2.0,
                                     in1=mn.rearrange("p (t h) -> p t h", h=HEADS), op0=ALU.mult, op1=ALU.add).then_inc(lf_ok, 1)
            dve.wait_ge(lft_ok, NCH)
            dve.wait_ge(one_ok, 2)
            dve.tensor_tensor_scan(run[:, 0:SEQ], ones[:, 0:SEQ], lft[:, 0:SEQ], 0.0, ALU.mult, ALU.add).then_inc(run_ok, 1)
            dve.tensor_tensor_scan(run[:, T:TC], ones[:, T:TC], lft[:, T:TC], 0.0, ALU.mult, ALU.add).then_inc(run_ok, 1)
            dve.wait_ge(run_ok, 2)
            dve.tensor_tensor_scan(run[:, SEQ:T], ones[:, SEQ:T], lft[:, SEQ:T], run[:, TC - 1:TC], ALU.mult,
                                   ALU.add).then_inc(run_ok, 1)
            dve.wait_ge(run_ok, 3)
            dve.tensor_copy(hi_r[:, :], run[:, :]).then_inc(run_ok, 1)
            dve.wait_ge(run_ok, 4)
            dve.tensor_tensor(run_lo[:, :], run[:, :], raw(hi_r[:, :]), ALU.subtract).then_inc(part_ok, 1)
            dve.tensor_scalar(neg_hi[:, :], raw(hi_r[:, :]), -1.0, None, ALU.mult).then_inc(part_ok, 1)
            dve.tensor_tensor(neg_lo[:, :], raw(hi_r[:, :]), run[:, :], ALU.subtract).then_inc(part_ok, 1)


def stage_tiles(nc, io, keep, dram, hhi, hlo):
    TILES = [base + i * P for base in (COL_U, COL_PG, COL_AG, COL_K, COL_Q) for i in range(4)]
    U0, PG0, AG0, K0, Q0 = 0, 4, 8, 12, 16
    PARTS = [(p * 512, 512) for p in range(4)] + [(SEQ, DEC)]
    with Scope(nc, "til") as s:
        acc = [s.ps(f"acc{c}", [P, 512]) for c in range(NCH)]
        full, free = s.sem("full"), s.sem("free")
        spt = s.sb("spt", [P, GROUPS, HIST])
        stage_forget(nc, io, keep, dram, hhi, hlo, acc, full, free, spt)
        with Scope(nc, "out") as o:
            wraw = o.sb("wraw", [P, KT, P])
            whi = [o.sb(f"whi{n}", [P, KT, P], F32R) for n in range(2)]
            wlo = [o.sb(f"wlo{n}", [P, KT, P], F32R) for n in range(2)]
            of = [o.sb(f"of{c}", [P, 512]) for c in range(NCH)]
            ohi = [o.sb(f"ohi{c}", [P, 512], F32R) for c in range(NCH)]
            olo = [o.sb(f"olo{c}", [P, 512], F32R) for c in range(NCH)]
            ub = o.sb("ub", [P, HIST + 512])
            sa = o.sb("sa", [P, HIST + 512])
            sb_ = o.sb("sb", [P, HIST + 512])
            dhi = o.sb("dhi", [P, 512], F32R)
            dlo = o.sb("dlo", [P, 512], F32R)
            early = o.sb("early", [P, GROUPS, HIST + 1])
            slot0 = o.sb("slot0", [P, 2])
            zeros = o.sb("zeros", [P, KT, P])
            w_in, w_hi, w_lo = o.sem("w_in"), o.sem("w_hi"), o.sem("w_lo")
            hi_ok = o.sem("hi_ok")
            out_f = [o.sem(f"out_f{c}") for c in range(NCH)]
            out_s = [o.sem(f"out_s{c}") for c in range(NCH)]
            u_in, u_out, pl, early_ok, dstep, zero_ok = o.sem("u_in"), o.sem("u_out"), o.sem("pl"), o.sem("early_ok"), o.sem("dstep"), o.sem("zero_ok")
            block = o.enter_context(nc.Block())
            wv = io["w_in"][0].rearrange("(k p) n -> p k n", p=P)

            @block.sync
            def _(sp):
                for n, col in enumerate(TILES):
                    if n >= 1:
                        sp.wait_ge(w_lo, n)
                    sp.dma_start(wraw[:, :, :], wv[:, :, col:col + P]).then_inc(w_in, 16)
                    for i in range(max(0, (n - 5) * 3), min(20, (n - 4) * 3)):
                        g, p = divmod(i, len(PARTS))
                        p0, w = PARTS[p]
                        for c in range(NCH):
                            sp.wait_ge(out_f[c], 16 * (g + 2))
                        if i >= 1:
                            sp.wait_ge(pl, i)
                        h = HIST if 0 < p < 4 else 0
                        sp.dma_start(ub[:, HIST - h:HIST + w], dram["u"][g, :, p0 - h:p0 + w]).then_inc(u_in, 16)
                        sp.wait_ge(pl, i + 1)
                        sp.dma_start(dram["d"][0, g, :, p0:p0 + w], raw(dhi[:, 0:w])).then_inc(u_out, 16)
                        sp.dma_start(dram["d"][1, g, :, p0:p0 + w], raw(dlo[:, 0:w])).then_inc(u_out, 16)
                sp.wait_ge(u_out, 32 * GROUPS * len(PARTS))

            @block.gpsimd
            def _(pool):
                pool.memset(zeros[:, :, :], 0.0).then_inc(zero_ok, 1)
                pool.wait_ge(zero_ok, 1)
                for c in range(NCH):
                    pool.memset(slot0[:, 0:1], 0.0).then_inc(out_f[c], 16)
                    pool.memset(slot0[:, 1:2], 0.0).then_inc(out_s[c], 32)
                    pool.wait_ge(out_f[c], 16)
                    pool.wait_ge(out_s[c], 32)
                for g, w in enumerate(WINDOWS):
                    for t in range(HIST + 1):
                        pool.memset(early[:, g, t:t + 1], w / min(t + 1, w)).then_inc(early_ok, 1)
                with pool.Fori(0, len(TILES) // 2) as m:
                    for b in range(2):
                        n = 2 * m + b
                        pool.wait_ge(w_in, 16 * n + 16)
                        pool.wait_ge(full, NCH * 2 * m + (1 if b == 0 else NCH))
                        pool.tensor_tensor(whi[b][:, :, :], wraw[:, :, :], zeros[:, :, :], ALU.add).then_inc(w_hi, 1)
                        pool.wait_ge(w_hi, n + 1)
                        pool.tensor_tensor(wlo[b][:, :, :], wraw[:, :, :], raw(whi[b][:, :, :]),
                                           ALU.subtract).then_inc(w_lo, 1)

            @block.tensor
            def _(pe):
                with pe.Fori(0, len(TILES) // 2) as m:
                    for b in range(2):
                        pe.wait_ge(w_lo, 2 * m + b + 1)
                        for c, (c0, n) in enumerate(CHUNKS):
                            pe.wait_ge(free, NCH * 2 * m + NCH * b + c + 1)
                            for k in range(KT):
                                pe.matmul(acc[c][:, 0:n], whi[b][:, k, :], hhi[:, k, c0:c0 + n], start=(k == 0), stop=False)
                                pe.matmul(acc[c][:, 0:n], wlo[b][:, k, :], hhi[:, k, c0:c0 + n], start=False, stop=False)
                                mm = pe.matmul(acc[c][:, 0:n], whi[b][:, k, :], hlo[:, k, c0:c0 + n],
                                               start=False, stop=(k == KT - 1))
                            mm.then_inc(full, 1)

            @block.scalar
            def _(act):
                def each_tile(first, body, stores):
                    with act.Fori(0, 4) as i:
                        for c in range(NCH + 1):
                            if c < NCH:
                                act.wait_ge(full, NCH * i + NCH * (first + 1) + c + 1)
                                body(i, c, CHUNKS[c][1])
                            if c >= 1:
                                act.wait_ge(free, NCH * i + NCH * (first + 1) + c)
                                stores(i, c - 1, *CHUNKS[c - 1])

                def plain(base, func):
                    def body(i, c, n):
                        act.wait_ge(out_f[c], 16 * i + 16 * (base + 1))
                        act.activation(of[c][:, 0:n], acc[c][:, 0:n], func).then_inc(free, 1)
                    return body

                def store_f(name):
                    def stores(i, c, c0, n):
                        act.dma_start(dram[name][i, :, c0:c0 + n], of[c][:, 0:n]).then_inc(out_f[c], 16)
                    return stores

                def split_k(i, c, n):
                    act.wait_ge(out_f[c], 16 * i + 16 * 13)
                    act.activation(of[c][:, 0:n], acc[c][:, 0:n], ACT.Copy)
                    act.wait_ge(out_s[c], 32 * i + 32)
                    act.activation(ohi[c][:, 0:n], acc[c][:, 0:n], ACT.Copy).then_inc(hi_ok, 1)

                def split_q(i, c, n):
                    act.wait_ge(out_s[c], 32 * i + 32 * 5)
                    act.activation(ohi[c][:, 0:n], acc[c][:, 0:n], ACT.Copy, scale=SCALE).then_inc(hi_ok, 1)

                def store_s(name, full_too):
                    def stores(i, c, c0, n):
                        act.dma_start(dram[name][i, 0, :, c0:c0 + n], raw(ohi[c][:, 0:n])).then_inc(out_s[c], 16)
                        act.dma_start(dram[name][i, 1, :, c0:c0 + n], raw(olo[c][:, 0:n])).then_inc(out_s[c], 16)
                        if full_too:
                            act.dma_start(dram["kf"][i, :, c0:c0 + n], of[c][:, 0:n]).then_inc(out_f[c], 16)
                    return stores

                each_tile(U0, plain(0, ACT.Copy), store_f("u"))
                each_tile(PG0, plain(4, ACT.Silu), store_f("pg"))
                each_tile(AG0, plain(8, ACT.Silu), store_f("ag"))
                each_tile(K0, split_k, store_s("k", True))
                each_tile(Q0, split_q, store_s("q", False))
                for c in range(NCH):
                    act.wait_ge(out_f[c], 16 * 17)
                    act.wait_ge(out_s[c], 32 * 9)

            @block.vector
            def _(dve):
                count = 0

                def step(ins):
                    nonlocal count
                    count += 1
                    ins.then_inc(dstep, 1)
                    dve.wait_ge(dstep, count)

                def pool_part(g, p, p0, w):
                    i = g * len(PARTS) + p
                    win = WINDOWS[g]
                    if p == 0:
                        step(dve.memset(ub[:, 0:HIST], 0.0))
                    if p == len(PARTS) - 1:
                        step(dve.tensor_copy(ub[:, 0:HIST], spt[:, g, :]))
                    dve.wait_ge(u_in, 16 * (i + 1))
                    src, n, end = ub, 1, HIST + w
                    bufs = [sa, sb_]
                    while n < win:
                        dst = bufs[0]
                        step(dve.tensor_tensor(dst[:, 2 * n - 1:end], src[:, 2 * n - 1:end], src[:, n - 1:end - n], ALU.add))
                        src, n, bufs = dst, 2 * n, bufs[::-1]
                    if p == 0:
                        step(dve.tensor_tensor(src[:, HIST:HIST + win - 1], src[:, HIST:HIST + win - 1],
                                               early[:, g, 0:win - 1], ALU.mult))
                    d = bufs[0][:, 0:w]
                    step(dve.scalar_tensor_tensor(out=d, in0=src[:, HIST:end], scalar=1.0 / win, in1=ub[:, HIST:end],
                                                  op0=ALU.mult, op1=ALU.subtract))
                    if i >= 1:
                        dve.wait_ge(u_out, 32 * i)
                    step(dve.tensor_copy(dhi[:, 0:w], d))
                    dve.tensor_tensor(dlo[:, 0:w], d, raw(dhi[:, 0:w]), ALU.subtract).then_inc(pl, 1)
                    dve.wait_ge(pl, i + 1)

                dve.wait_ge(early_ok, GROUPS * (HIST + 1))
                for g in range(GROUPS):
                    for p, (p0, w) in enumerate(PARTS):
                        pool_part(g, p, p0, w)
                for first, scale in ((K0, 1.0), (Q0, SCALE)):
                    with dve.Fori(0, 4) as i:
                        for c, (_, n) in enumerate(CHUNKS):
                            dve.wait_ge(hi_ok, NCH * i + NCH * (first - K0) + c + 1)
                            dve.scalar_tensor_tensor(out=olo[c][:, 0:n], in0=acc[c][:, 0:n], scalar=scale,
                                                     in1=raw(ohi[c][:, 0:n]), op0=ALU.mult, op1=ALU.subtract).then_inc(free, 1)


def stage_pool(nc, io, keep, dram):
    NT = NQ + 1
    with Scope(nc, "pol") as s:
        wp = s.sb("wp", [P, GROUPS, P])
        wphi = s.sb("wphi", [P, GROUPS, P], F32R)
        wplo = s.sb("wplo", [P, GROUPS, P], F32R)
        dh = s.sb("dh", [P, GROUPS, T], F32R)
        dl = s.sb("dl", [P, GROUPS, T], F32R)
        pg = s.sb("pg", [P, GROUPS, T])
        kf = s.sb("kf", [P, PAIRS, T])
        ul = s.sb("ul", [P, 2, GROUPS, HIST])
        zf = s.sb("zf", [P, 2, 512])
        zhi = s.sb("zhi", [P, 2, 512], F32R)
        zlo = s.sb("zlo", [P, 2, 512], F32R)
        krow = s.sb("krow", [P, 2, 512])
        urow = s.sb("urow", [HIST, 2, A])
        acc = [s.ps(f"acc{n}", [P, 512]) for n in range(2)]
        kps = [s.ps(f"kps{n}", [P, 512]) for n in range(2)]
        ups = [s.ps(f"ups{n}", [P, 512]) for n in range(2)]
        wp_in, ul_in = s.sem("wp_in"), s.sem("ul_in")
        d_in = [s.sem(f"d_in{g}") for g in range(GROUPS)]
        k_in = s.sem("k_in")
        w_lo, full, zf_ok, zhi_ok, zlo_ok = (s.sem(n) for n in ("w_lo", "full", "zf_ok", "zhi_ok", "zlo_ok"))
        z_out = [s.sem(f"z_out{n}") for n in range(2)]
        k_out = [s.sem(f"k_out{n}") for n in range(2)]
        u_turn, u_row, u_out, k_turn, k_row = (s.sem(n) for n in ("u_turn", "u_row", "u_out", "k_turn", "k_row"))
        block = s.enter_context(nc.Block())
        ident = keep["ident"]
        WORK = [(g, c) for g in range(GROUPS) for c in range(NCH)]

        @block.sync
        def _(sp):
            sp.dma_start(wp[:, :, :], io["w_pool"][0].rearrange("g c d -> c g d")).then_inc(wp_in, 16)
            for g in range(GROUPS):
                sp.dma_start(raw(dh[:, g, :]), dram["d"][0, g]).then_inc(d_in[g], 16)
                sp.dma_start(raw(dl[:, g, :]), dram["d"][1, g]).then_inc(d_in[g], 16)
                sp.dma_start(pg[:, g, :], dram["pg"][g]).then_inc(d_in[g], 16)
            for i, (g, c) in enumerate(WORK):
                c0, n = CHUNKS[c]
                sp.wait_ge(zlo_ok, i + 1)
                for part, z in enumerate((zhi, zlo)):
                    sp.dma_start(dram["z"][part, PAIRS + g, :, c0:c0 + n], raw(z[:, i % 2, 0:n])).then_inc(z_out[i % 2], 16)
            for n in range(2):
                sp.wait_ge(z_out[n], 32 * len(WORK[n::2]))

        @block.scalar
        def _(act):
            for p in range(PAIRS):
                act.dma_start(kf[:, p, :], dram["kf"][p]).then_inc(k_in, 16)
            for n, end in enumerate((SEQ, T)):
                act.dma_start(ul[:, n, :, :], dram["u"][:, :, end - HIST:end].rearrange("g p c -> p g c")).then_inc(ul_in, 16)
            work = list(enumerate(WORK))
            for t in range(max(NT, len(work))):
                if t < len(work):
                    i, (g, c) = work[t]
                    n = CHUNKS[c][1]
                    act.wait_ge(zf_ok, i + 1)
                    if i >= 2:
                        act.wait_ge(z_out[i % 2], 32 * (i // 2))
                    act.activation(zhi[:, i % 2, 0:n], zf[:, i % 2, 0:n], ACT.Copy).then_inc(zhi_ok, 1)
                if t < NT:
                    n = P if t < NQ else DEC
                    act.wait_ge(k_turn, t + 1)
                    if t >= 2:
                        act.wait_ge(k_out[t % 2], 16 * (t // 2))
                    act.activation(krow[0:n, t % 2, :], kps[t % 2][0:n, :], ACT.Copy).then_inc(k_row, 1)
            for n in range(2):
                act.wait_ge(u_turn, n + 1)
                act.activation(urow[:, n, :], ups[n][0:HIST, :], ACT.Copy).then_inc(u_row, 1)
            act.wait_ge(u_row, 2)
            act.dma_start(io["pool_prompt"][0, 0], urow[:, 0, :]).then_inc(u_out, 16)
            act.dma_start(io["pool_sample"][0, 0], urow[:, 1, :]).then_inc(u_out, 16)
            act.wait_ge(u_out, 32)

        @block.gpsimd
        def _(pool):
            for t in range(NT):
                n = P if t < NQ else DEC
                dst = io["k_prompt"][0, 0, t * P:(t + 1) * P] if t < NQ else io["k_sample"][0, 0]
                pool.wait_ge(k_row, t + 1)
                pool.dma_start(dst.rearrange("s h d -> s (h d)"), krow[0:n, t % 2, :]).then_inc(k_out[t % 2], 16)
            for n in range(2):
                pool.wait_ge(k_out[n], 16 * len(range(n, NT, 2)))

        @block.tensor
        def _(pe):
            work = list(enumerate(WORK))
            pe.wait_ge(k_in, 64)
            for t in range(max(NT, len(work))):
                if t < NT:
                    n = P if t < NQ else DEC
                    if t >= 2:
                        pe.wait_ge(k_row, t - 1)
                    for p in range(PAIRS):
                        mm = pe.transpose(kps[t % 2][0:n, p * P:(p + 1) * P], kf[:, p, t * P:t * P + n], ident[:, :])
                    mm.then_inc(k_turn, 1)
                if t < len(work):
                    i, (g, c) = work[t]
                    c0, n = CHUNKS[c]
                    pe.wait_ge(w_lo, 2)
                    pe.wait_ge(d_in[g], 48)
                    if i >= 2:
                        pe.wait_ge(zf_ok, i - 1)
                    pe.matmul(acc[i % 2][:, 0:n], wphi[:, g, :], dh[:, g, c0:c0 + n], start=True, stop=False)
                    pe.matmul(acc[i % 2][:, 0:n], wplo[:, g, :], dh[:, g, c0:c0 + n], start=False, stop=False)
                    pe.matmul(acc[i % 2][:, 0:n], wphi[:, g, :], dl[:, g, c0:c0 + n], start=False, stop=True).then_inc(full, 1)
            pe.wait_ge(ul_in, 32)
            for n in range(2):
                for g in range(GROUPS):
                    mm = pe.transpose(ups[n][0:HIST, g * P:(g + 1) * P], ul[:, n, g, :], ident[:, :])
                mm.then_inc(u_turn, 1)

        @block.vector
        def _(dve):
            dve.wait_ge(wp_in, 16)
            dve.tensor_copy(wphi[:, :, :], wp[:, :, :]).then_inc(w_lo, 1)
            dve.wait_ge(w_lo, 1)
            dve.tensor_tensor(wplo[:, :, :], wp[:, :, :], raw(wphi[:, :, :]), ALU.subtract).then_inc(w_lo, 1)
            for i, (g, c) in enumerate(WORK):
                c0, n = CHUNKS[c]
                dve.wait_ge(full, i + 1)
                dve.wait_ge(d_in[g], 48)
                if i >= 2:
                    dve.wait_ge(zlo_ok, i - 1)
                dve.scalar_tensor_tensor(out=zf[:, i % 2, 0:n], in0=acc[i % 2][:, 0:n],
                                         scalar=keep["cols"][:, ROW_PS + g:ROW_PS + g + 1], in1=pg[:, g, c0:c0 + n],
                                         op0=ALU.mult, op1=ALU.mult).then_inc(zf_ok, 1)
                dve.wait_ge(zhi_ok, i + 1)
                dve.tensor_tensor(zlo[:, i % 2, 0:n], zf[:, i % 2, 0:n], raw(zhi[:, i % 2, 0:n]), ALU.subtract).then_inc(zlo_ok, 1)


class Row:

    def __init__(self, tile):
        self.tile, self.dec = tile, tile == NQ
        self.m = DEC if self.dec else P
        self.q0 = tile * P
        keys = (tile + 1) * P
        self.chunks = [(SEQ, DEC + PAST)] if self.dec else [(k, min(512, keys - k)) for k in range(0, keys, 512)]
        self.mask0 = 0 if self.dec else (tile % 4) * P


class Unit:

    def __init__(self, out, q0, width, tile, key0, keys, skip, masked):
        self.out, self.q0, self.width = out, q0, width
        self.tile, self.key0, self.keys = tile, key0, keys
        self.skip, self.masked = skip, masked
        self.n = width - skip
        self.first = self.last = False


def attention_units():
    units = []
    for out, c in enumerate(reversed(range(4))):
        for kt in range(4 * c + 4):
            skip = max(0, kt - 4 * c) * P
            units.append(Unit(out, c * 512, 512, kt, kt * P, P, skip, kt >= 4 * c))
    units.append(Unit(4, SEQ, DEC, NQ + 1, T, PAST, 0, False))
    units.append(Unit(4, SEQ, DEC, NQ, SEQ, DEC, 0, True))
    for n, u in enumerate(units):
        u.first = n == 0 or units[n - 1].out != u.out
        u.last = n == len(units) - 1 or units[n + 1].out != u.out
    return units


ROWS = [Row(t) for t in range(NQ + 1)]
MAXIMA = [(r, c) for r in ROWS for c in range(len(r.chunks))]
UNITS = attention_units()
NR, NA, NB, NO = len(ROWS), len(MAXIMA), len(UNITS), 5
SUM_TO = 12
DVE_SUMS = [n for n in range(1, SUM_TO, 2)]
POOL_SUMS = [n for n in range(NB) if n not in DVE_SUMS]
ND, NP = len(DVE_SUMS), len(POOL_SUMS)
W_RING = 6
SPLIT_LAG = 2
LAG = 4
A_FROM, A_TO = 12, 36


def den_tiles(u):
    return max(1, u.width // P)


def step_events(cur, nxt, prev, gate):
    ev = []
    done = 0
    for u in range(NB if cur else 0):
        if u >= SPLIT_LAG:
            ev.append(("split", 0, u - SPLIT_LAG))
        elif prev:
            ev.append(("split", -1, NB + u - SPLIT_LAG))
        ev.append(("score", 0, u))
        if nxt and u >= A_FROM:
            upto = min(NA, -(-NA * (u + 1 - A_FROM) // (A_TO - A_FROM)))
            while done < upto:
                ev.append(("max", 1, done))
                done += 1
        if u == A_TO and nxt:
            ev.append(("row_max", 1, 0))
        if u == A_TO + 1 and nxt:
            ev.append(("max_split", 1, 0))
        v, d = (u - LAG, 0) if u >= LAG else (NB + u - LAG, -1)
        if d == 0 or prev:
            ev.append(("value", d, v))
            if UNITS[v].last:
                ev.append(("out", d, UNITS[v].out))
        for n in range(2, 6):
            v, d = (u - LAG - n, 0) if u >= LAG + n else (NB + u - LAG - n, -1)
            t = n - (2 if den_tiles(UNITS[v]) > 1 else 4)
            if (d == 0 or prev) and UNITS[v].last and 0 <= t < den_tiles(UNITS[v]):
                ev.append(("den", d, (UNITS[v].out, t)))
        if prev and u == LAG + 4:
            ev.append(("rec", -1, 0))
        if prev and u == LAG + 5:
            ev.append(("rec_row", -1, 0))
        if gate and u >= 13 and (u - 13) % 5 == 0 and (u - 13) // 5 < NO:
            ev.append(("gate", 0, (u - 13) // 5))
        if gate and u >= 16 and (u - 16) % 5 == 0 and (u - 16) // 5 < NO:
            ev.append(("gate_split", 0, (u - 16) // 5))
    if not cur:
        ev += [("max", 1, k) for k in range(NA)] + [("row_max", 1, 0), ("max_split", 1, 0)]
    return ev


def last_events():
    ev = [("split", 0, n) for n in range(NB - SPLIT_LAG, NB)]
    for v in range(NB - LAG, NB):
        ev.append(("value", 0, v))
        if UNITS[v].last:
            ev.append(("out", 0, UNITS[v].out))
    ev += [("den", 0, (UNITS[v].out, t)) for v in range(NB - LAG - 5, NB) if UNITS[v].last
           for t in range(max(0, NB - LAG - 2 - v), den_tiles(UNITS[v]))]
    ev += [("rec", 0, 0), ("rec_row", 0, 0)]
    for c in range(NO):
        ev.append(("last_gate", 0, c))
        if c >= 1:
            ev.append(("gate_split", 0, c - 1))
    return ev + [("gate_split", 0, NO - 1)]


ROUNDS = PAIRS - 1
FIRST = step_events(False, True, False, False)
HEAD0 = step_events(True, True, False, False)
ODD_HEAD = step_events(True, True, True, False)
EVEN_HEAD = step_events(True, True, True, True)
LAST = step_events(True, False, True, False) + last_events()


class At:

    def __init__(self, j, o):
        self.j, self.o = j, o

    def __call__(self, d, per, k):
        return 2 * per * self.j + per * (self.o + d) + k

    def slot(self, d, per, k, size):
        return (per * (self.o + d) + k) % size


def walk(eng, emit):
    emit(FIRST, At(0, -1))
    emit(HEAD0, At(0, 0))
    with eng.Fori(0, ROUNDS) as j:
        emit(ODD_HEAD, At(j, 1))
        emit(EVEN_HEAD, At(j, 2))
    emit(LAST, At(ROUNDS, 1))


def stage_attend(nc, io, keep, dram):
    S_RING, A_RING, O_RING, ACC_RING = 3, 2, 2, 2
    KQ = DH + 4
    KM = KQ + 2

    with Scope(nc, "att") as s:
        qa = [s.sb(f"qa{e}", [P, T], F32R) for e in range(2)]
        qb = [s.sb(f"qb{e}", [KM, T], F32R) for e in range(2)]
        ka = [s.sb(f"ka{e}", [P, TC], F32R) for e in range(2)]
        kb = [s.sb(f"kb{e}", [KM, TC], F32R) for e in range(2)]
        vt = [s.sb(f"vt{e}", [P, NQ + 2, P], F32R) for e in range(2)]
        w = [s.sb(f"w{n}", [P, 512]) for n in range(W_RING)]
        whi = [s.sb(f"whi{n}", [P, 512], F32R) for n in range(W_RING)]
        wlo = [s.sb(f"wlo{n}", [P, 512], F32R) for n in range(W_RING)]
        wsum = [s.sb(f"wsum{n}", [P, 512]) for n in range(ACC_RING)]
        dsum = s.sb("dsum", [P, 512])
        nmax = s.sb("nmax", [P, NR, 4])
        nrow = s.sb("nrow", [P, NR])
        msp = s.sb("msp", [NR, 2, P], F32R)
        rec = s.sb("rec", [P, NR])
        rdt = s.sb("rdt", [NR, P])
        tmp = s.sb("tmp", [P, 2, 512])
        att = s.sb("att", [P, T])
        rb = s.sb("rb", [P, T])
        ag = s.sb("ag", [P, T])
        zhi = s.sb("zhi", [P, T], F32R)
        zlo = s.sb("zlo", [P, T], F32R)
        zeros = s.sb("zeros", [P, 512])
        one = s.sb("one", [P, 1])
        start = s.sb("start", [P, 16])
        sps = [s.ps(f"sps{n}", [P, 512]) for n in range(S_RING)]
        aps = [s.ps(f"aps{n}", [P, 512]) for n in range(A_RING)]
        ops = [s.ps(f"ops{n}", [P, 512]) for n in range(O_RING)]
        mps = s.ps("mps", [P, 512])
        den_ps, max_ps, rec_ps = mps[:, 0:NR], mps[0:NR, P:2 * P], mps[0:NR, 2 * P:3 * P]
        qk_in = [s.sem(f"qk_in{e}") for e in range(2)]
        v_in = [s.sem(f"v_in{e}") for e in range(2)]
        m_in = [s.sem(f"m_in{e}") for e in range(2)]
        names = ("ready", "a_full", "a_free", "row_ok", "max_turned", "max_hi", "max_lo", "m_out", "s_full", "exp_ok",
                 "hi_ok", "lo_ok", "sum_ok", "dsum_ok", "val_ok", "low_out", "out_ok", "den_ok", "rec_ok", "rec_turned", "row_out",
                 "rd_out", "g_in", "g_mul", "g_z", "g_hi", "g_lo", "z_out")
        (ready, a_full, a_free, row_ok, max_turned, max_hi, max_lo, m_out, s_full, exp_ok,
         hi_ok, lo_ok, sum_ok, dsum_ok, val_ok, low_out, out_ok, den_ok, rec_ok, rec_turned, row_out,
         rd_out, g_in, g_mul, g_z, g_hi, g_lo,z_out) = (s.sem(n) for n in names)
        free_at_start = [(a_free, A_RING), (exp_ok, S_RING), (lo_ok, W_RING), (val_ok, W_RING),
                         (out_ok, O_RING), (den_ok, ACC_RING), (row_ok, 1), (rec_ok, 2), (m_out, 32), (rd_out, 32),
                         (g_lo, NO), (z_out, 32)]
        QK, V = 16 * 9, 16 * 3
        block = s.enter_context(nc.Block())

        def gate_cols(i):
            u = next(u for u in UNITS if u.out == i)
            return slice(u.q0, u.q0 + u.width)

        def multiply_gate(eng, at, i):
            cols = gate_cols(i)
            if i == 0:
                eng.wait_ge(g_in, 48 * at.j + 48)
                eng.wait_ge(out_ok, 2 * NO * at.j + 2 * NO + O_RING)
            eng.tensor_tensor(ag[:, cols], rb[:, cols], ag[:, cols], ALU.mult).then_inc(g_mul, 1)
            eng.wait_ge(g_mul, NO * at.j + i + 1)
            eng.tensor_tensor(rb[:, cols], ag[:, cols], att[:, cols], ALU.mult).then_inc(g_z, 1)

        def wait_sum(eng, at, d, i):
            if i < 0:
                d, i = d - 1, i + NB
            if at.o + d < 0:
                return
            if i in DVE_SUMS:
                eng.wait_ge(dsum_ok, at(d, ND, DVE_SUMS.index(i) + 1))
            else:
                eng.wait_ge(sum_ok, at(d, NP, POOL_SUMS.index(i) + 1))

        def halves(e):
            return (slice(0, DH), slice(DH, P)) if e == 0 else (slice(DH, P), slice(0, DH))

        def load_qk(sp, h, pair, e):
            lo, hi = e * DH, (e + 1) * DH
            q, k = dram["q"], dram["k"]
            for dst, src in ((qa[e][0:DH, :], q[pair, 0, lo:hi, :]), (qa[e][DH:P, :], q[pair, 1, lo:hi, :]),
                             (ka[e][0:DH, :], k[pair, 0, lo:hi, :]), (ka[e][DH:P, :], k[pair, 0, lo:hi, :]),
                             (qb[e][0:DH, :], q[pair, 0, lo:hi, :]), (qb[e][DH:KQ, :], dram["fq"][h, :, 0:T]),
                             (kb[e][0:DH, :], k[pair, 1, lo:hi, :]), (kb[e][DH:KQ, :], dram["fk"][h, :, :]),
                             (kb[e][KQ:KM, :], dram["fk"][h, 0:3:2, :])):
                sp.dma_start(raw(dst), src).then_inc(qk_in[e], 16)

        def load_v(sp, h, e):
            v = dram["v"][:, :, bass.ts(h, P)]
            sp.dma_start(raw(vt[e][0:DEC, :, :]), v[:, 0:DEC].rearrange("t p c -> p t c")).then_inc(v_in[e], 16)
            for a, b in ((0, NQ), (NQ + 1, NQ + 2)):
                sp.dma_start(raw(vt[e][DEC:P, a:b, :]), v[a:b, DEC:P].rearrange("t p c -> p t c")).then_inc(v_in[e], 16)

        def max_rows(sp, at, e, h):
            sp.wait_ge(max_lo, at(0, 1, 1))
            sp.dma_start(dram["m"][h, :, 0:SEQ].rearrange("a (t q) -> t a q", q=P), raw(msp[0:NQ, :, :])).then_inc(m_out, 16)
            sp.dma_start(dram["m"][h, :, SEQ:T].rearrange("a (t q) -> t a q", q=DEC), raw(msp[NQ:NR, :, 0:DEC])).then_inc(m_out, 16)
            sp.wait_ge(m_out, at(0, 32, 64))
            sp.dma_start(raw(qb[e][KQ:KM, :]), dram["m"][h]).then_inc(m_in[e], 16)

        def rec_out(sp, at, h):
            sp.wait_ge(row_out, at(0, 1, 1))
            sp.dma_start(dram["rden"][h, 0:SEQ].rearrange("(t q) -> t q", q=P), rdt[0:NQ, :]).then_inc(rd_out, 16)
            sp.dma_start(dram["rden"][h, SEQ:T].rearrange("(t q) -> t q", q=DEC), rdt[NQ:NR, 0:DEC]).then_inc(rd_out, 16)

        def gate_in(sp, pair):
            sp.wait_ge(g_lo, NO * pair + NO)
            sp.dma_start(ag[:, :], dram["ag"][pair]).then_inc(g_in, 16)
            sp.wait_ge(rd_out, 64 * pair + 96)
            for e in range(2):
                sp.dma_start(rb[halves(e)[0], :], dram["rden"][2 * pair + e].partition_broadcast(DH)).then_inc(g_in, 16)

        def gate_out(sp, pair):
            sp.wait_ge(g_lo, NO * pair + 2 * NO)
            for part, z in enumerate((zhi, zlo)):
                sp.dma_start(dram["z"][part, pair], raw(z[:, :])).then_inc(z_out, 16)

        @block.sync
        def _(sp):
            load_qk(sp, 0, 0, 0)
            load_v(sp, 0, 0)
            load_qk(sp, 1, 0, 1)
            load_v(sp, 1, 1)
            sp.wait_ge(ready, 5)
            max_rows(sp, At(0, 0), 0, 0)
            max_rows(sp, At(0, 1), 1, 1)
            with sp.Fori(0, ROUNDS) as j:
                for o in (1, 2):
                    at = At(j, o)
                    e = (o + 1) % 2
                    sp.wait_ge(s_full, at(0, NB, 0))
                    load_qk(sp, 2 * j + o + 1, j + 1, e)
                    sp.wait_ge(val_ok, at(0, NB, W_RING))
                    load_v(sp, 2 * j + o + 1, e)
                    rec_out(sp, At(j, o - 1), 2 * j + o - 1)
                    if o == 2:
                        gate_in(sp, j)
                    max_rows(sp, At(j, o + 1), e, 2 * j + o + 1)
                    if o == 2:
                        gate_out(sp, j)
            rec_out(sp, At(ROUNDS, 0), 2 * ROUNDS)
            rec_out(sp, At(ROUNDS, 1), 2 * ROUNDS + 1)
            gate_in(sp, ROUNDS)
            for i in range(NO):
                cols = gate_cols(i)
                sp.wait_ge(g_lo, NO * PAIRS + i + 1)
                for part, z in enumerate((zhi, zlo)):
                    sp.dma_start(dram["z"][part, ROUNDS, :, cols], raw(z[:, cols])).then_inc(z_out, 16)
            sp.wait_ge(z_out, 32 * PAIRS + 32 * NO)

        @block.tensor
        def _(pe):
            def emit(events, at):
                for kind, d, i in events:
                    e = (at.o + d) % 2
                    if kind == "max":
                        r, c = MAXIMA[i]
                        k0, n = r.chunks[c]
                        if i == 0:
                            pe.wait_ge(qk_in[e], QK * at.j + QK * ((at.o + d) // 2 + 1))
                        pe.wait_ge(a_free, at(d, NA, i + 1))
                        bank = aps[at.slot(d, NA, i, A_RING)]
                        masked = c == len(r.chunks) - 1
                        q = slice(r.q0, r.q0 + r.m)
                        pe.matmul(bank[0:r.m, 0:n], qa[e][:, q], ka[e][:, k0:k0 + n], start=True, stop=False)
                        mm = pe.matmul(bank[0:r.m, 0:n], qb[e][0:KQ, q], kb[e][0:KQ, k0:k0 + n], start=False, stop=not masked)
                        if masked:
                            mm = pe.matmul(bank[0:r.m, r.mask0:r.mask0 + r.m], keep["identb"][0:r.m, 0:r.m],
                                           keep["mask"][0:r.m, 0:r.m], start=False, stop=True)
                        mm.then_inc(a_full, 1)
                    elif kind == "max_split":
                        pe.wait_ge(row_ok, at(d, 1, 2))
                        pe.transpose(max_ps, nrow[:, :], keep["ident"][:, :]).then_inc(max_turned, 1)
                    elif kind == "score":
                        u = UNITS[i]
                        if i == 0:
                            pe.wait_ge(m_in[e], 16 * at.j + 16 * ((at.o + d) // 2 + 1))
                        pe.wait_ge(exp_ok, at(d, NB, i + 1))
                        bank = sps[at.slot(d, NB, i, S_RING)]
                        out = bank[0:u.keys, 0:u.n]
                        k, q = slice(u.key0, u.key0 + u.keys), slice(u.q0 + u.skip, u.q0 + u.width)
                        pe.matmul(out, ka[e][:, k], qa[e][:, q], start=True, stop=False)
                        mm = pe.matmul(out, kb[e][:, k], qb[e][:, q], start=False, stop=not u.masked)
                        if u.masked:
                            m = u.keys
                            mm = pe.matmul(bank[0:m, 0:m], keep["mask"][0:m, 0:m], keep["identb"][0:m, 0:m], start=False, stop=True)
                        mm.then_inc(s_full, 1)
                    elif kind == "value":
                        u = UNITS[i]
                        if i == 0:
                            pe.wait_ge(v_in[e], V * at.j + V * ((at.o + d) // 2 + 1))
                        if u.first:
                            pe.wait_ge(out_ok, at(d, NO, u.out + 1))
                        pe.wait_ge(lo_ok, at(d, NB, i + 1 + W_RING))
                        bank = ops[at.slot(d, NO, u.out, O_RING)]
                        b = at.slot(d, NB, i, W_RING)
                        for part in (whi, wlo):
                            mm = pe.matmul(bank[:, u.skip:u.width], vt[e][0:u.keys, u.tile, :], part[b][0:u.keys, 0:u.n],
                                           start=(u.first and part is whi), stop=(u.last and part is wlo))
                        mm.then_inc(val_ok, 1)
                    elif kind == "den":
                        out, t = i
                        last = [n for n, u in enumerate(UNITS) if u.out == out][-1]
                        u = UNITS[last]
                        if t == 0:
                            wait_sum(pe, at, d, last)
                            if out == 0:
                                pe.wait_ge(rec_ok, at(d, 2, 2))
                                if ND:
                                    wait_sum(pe, at, d, DVE_SUMS[-1])
                        m, col = min(P, u.width), u.q0 // P + t
                        extra = out == 0 and ND
                        cols = slice(t * P, t * P + m)
                        dst = den_ps[0:m, col:col + 1]
                        mm = pe.matmul(dst, wsum[at.slot(d, NO, out, ACC_RING)][:, cols], one[:, :], start=True, stop=not extra)
                        if extra:
                            mm = pe.matmul(dst, dsum[:, cols], one[:, :], start=False, stop=True)
                        if t == den_tiles(u) - 1:
                            mm.then_inc(den_ok, 1)
                    elif kind == "rec_row":
                        pe.wait_ge(rec_ok, at(d, 2, 4))
                        pe.transpose(rec_ps, rec[:, :], keep["ident"][:, :]).then_inc(rec_turned, 1)

            pe.wait_ge(ready, 5)
            walk(pe, emit)

        @block.scalar
        def _(act):
            def emit(events, at):
                for kind, d, i in events:
                    if kind == "score":
                        u = UNITS[i]
                        act.wait_ge(s_full, at(d, NB, i + 1))
                        act.wait_ge(lo_ok, at(d, NB, i + 1))
                        wait_sum(act, at, d, i - W_RING)
                        act.activation(w[at.slot(d, NB, i, W_RING)][0:u.keys, 0:u.n],
                                       sps[at.slot(d, NB, i, S_RING)][0:u.keys, 0:u.n], ACT.Exp).then_inc(exp_ok, 1)
                    elif kind == "split":
                        u = UNITS[i]
                        b = at.slot(d, NB, i, W_RING)
                        act.wait_ge(exp_ok, at(d, NB, i + 1 + S_RING))
                        act.wait_ge(val_ok, at(d, NB, i + 1))
                        act.activation(whi[b][0:u.keys, 0:u.n], w[b][0:u.keys, 0:u.n], ACT.Copy).then_inc(hi_ok, 1)
                    elif kind == "out":
                        last = [n for n, u in enumerate(UNITS) if u.out == i][-1]
                        width = UNITS[last].width
                        b = at.slot(d, NO, i, O_RING)
                        main, low = halves((at.o + d) % 2)
                        act.wait_ge(val_ok, at(d, NB, last + 1 + W_RING))
                        act.wait_ge(out_ok, at(d, NO, i + 1))
                        act.activation(tmp[main, b, 0:width], ops[b][low, 0:width], ACT.Copy).then_inc(low_out, 1)
                    elif kind == "gate_split":
                        pair = at.j
                        cols = gate_cols(i)
                        act.wait_ge(g_z, NO * pair + i + 1)
                        if i == 0:
                            act.wait_ge(z_out, 32 * pair + 32)
                        act.activation(zhi[:, cols], rb[:, cols], ACT.Copy).then_inc(g_hi, 1)

            act.wait_ge(ready, 5)
            walk(act, emit)

        @block.vector
        def _(dve):
            def emit(events, at):
                for kind, d, i in events:
                    if kind == "max":
                        r, c = MAXIMA[i]
                        n = r.chunks[c][1]
                        dve.wait_ge(a_full, at(d, NA, i + 1))
                        if i == 0:
                            dve.wait_ge(row_ok, at(d, 1, 1))
                        dve.tensor_reduce(nmax[0:r.m, r.tile, c:c + 1], aps[at.slot(d, NA, i, A_RING)][0:r.m, 0:n], AX, ALU.max,
                                          negate=True).then_inc(a_free, 1)
                    elif kind == "row_max":
                        dve.wait_ge(a_free, at(d, NA, NA + A_RING))
                        if at.o >= 0:
                            dve.wait_ge(max_turned, at(d, 1, 0))
                        dve.tensor_reduce(nrow[:, :], nmax[:, :, :], AX, ALU.min).then_inc(row_ok, 1)
                    elif kind == "max_split":
                        dve.wait_ge(max_turned, at(d, 1, 1))
                        dve.wait_ge(m_out, at(d, 32, 32))
                        dve.tensor_copy(msp[:, 0, :], max_ps).then_inc(max_hi, 1)
                        dve.wait_ge(max_hi, at(d, 1, 1))
                        dve.tensor_tensor(msp[:, 1, :], max_ps, raw(msp[:, 0, :]), ALU.subtract).then_inc(max_lo, 1)
                    elif kind == "split":
                        u = UNITS[i]
                        b = at.slot(d, NB, i, W_RING)
                        dve.wait_ge(hi_ok, at(d, NB, i + 1))
                        dve.tensor_tensor(wlo[b][0:u.keys, 0:u.n], w[b][0:u.keys, 0:u.n], raw(whi[b][0:u.keys, 0:u.n]),
                                          ALU.subtract).then_inc(lo_ok, 1)
                        if i in DVE_SUMS:
                            n = DVE_SUMS.index(i)
                            if n == 0:
                                if at.o + d > 0:
                                    dve.wait_ge(den_ok, at(d - 1, NO, 1 + ACC_RING))
                                dve.tensor_copy(dsum[:, :], w[b][:, :]).then_inc(dsum_ok, 1)
                            else:
                                dve.wait_ge(dsum_ok, at(d, ND, n))
                                dve.tensor_tensor(dsum[:, :], dsum[:, :], w[b][:, :], ALU.add).then_inc(dsum_ok, 1)
                    elif kind == "out":
                        b = at.slot(d, NO, i, O_RING)
                        main, _ = halves((at.o + d) % 2)
                        cols = gate_cols(i)
                        width = cols.stop - cols.start
                        dve.wait_ge(low_out, at(d, NO, i + 1))
                        if at.o + d == 2:
                            dve.wait_ge(g_z, NO * at.j + i + 1)
                        elif at.o >= 1:
                            dve.wait_ge(g_lo, NO * at.j + NO)
                        dve.tensor_tensor(att[main, cols], ops[b][main, 0:width], tmp[main, b, 0:width], ALU.add).then_inc(out_ok, 1)
                    elif kind == "rec":
                        dve.wait_ge(den_ok, at(d, NO, NO + ACC_RING))
                        if at.o + d > 0:
                            dve.wait_ge(rec_turned, at(d, 1, 0))
                        dve.reciprocal(rec[:, 0:NQ], den_ps[:, 0:NQ]).then_inc(rec_ok, 1)
                        dve.reciprocal(rec[0:DEC, NQ:NR], den_ps[0:DEC, NQ:NR]).then_inc(rec_ok, 1)
                    elif kind == "rec_row":
                        dve.wait_ge(rec_turned, at(d, 1, 1))
                        dve.wait_ge(rd_out, at(d, 32, 32))
                        dve.tensor_copy(rdt[:, :], rec_ps).then_inc(row_out, 1)
                    elif kind == "last_gate":
                        multiply_gate(dve, at, i)
                    elif kind == "gate_split":
                        cols = gate_cols(i)
                        dve.wait_ge(g_hi, NO * at.j + i + 1)
                        dve.tensor_tensor(zlo[:, cols], rb[:, cols], raw(zhi[:, cols]), ALU.subtract).then_inc(g_lo, 1)

            dve.wait_ge(ready, 5)
            walk(dve, emit)

        @block.gpsimd
        def _(pool):
            pool.memset(zeros[:, :], 0.0).then_inc(ready, 1)
            pool.memset(one[:, :], 1.0).then_inc(ready, 1)
            pool.memset(nmax[:, :, :], -MASKED).then_inc(ready, 1)
            pool.memset(rec[:, :], 1.0).then_inc(ready, 1)
            pool.wait_ge(ready, 4)
            for n, (sem, size) in enumerate(free_at_start):
                pool.memset(start[:, n:n + 1], 0.0).then_inc(sem, size)
            pool.memset(start[:, 15:16], 0.0).then_inc(ready, 1)

            def emit(events, at):
                for kind, d, i in events:
                    if kind == "score":
                        u = UNITS[i]
                        src = w[at.slot(d, NB, i, W_RING)][0:u.keys, 0:u.n]
                        dst = wsum[at.slot(d, NO, u.out, ACC_RING)][0:u.keys, u.skip:u.width]
                        if i in DVE_SUMS:
                            continue
                        pool.wait_ge(exp_ok, at(d, NB, i + 1 + S_RING))
                        if u.first:
                            pool.wait_ge(den_ok, at(d, NO, u.out + 1))
                            pool.tensor_tensor(dst, src, zeros[0:u.keys, 0:u.n], ALU.add).then_inc(sum_ok, 1)
                        else:
                            pool.wait_ge(sum_ok, at(d, NP, POOL_SUMS.index(i)))
                            pool.tensor_tensor(dst, dst, src, ALU.add).then_inc(sum_ok, 1)
                    elif kind == "gate":
                        multiply_gate(pool, at, i)

            walk(pool, emit)


def stage_out(nc, io, keep, dram):
    NT = NQ + 1
    with Scope(nc, "fin") as s:
        wraw = s.sb("wraw", [P, KT, D])
        whi = s.sb("whi", [P, KT, D], F32R)
        wlo = s.sb("wlo", [P, KT, D], F32R)
        zh = [s.sb(f"zh{n}", [P, KT, P], F32R) for n in range(2)]
        zl = [s.sb(f"zl{n}", [P, KT, P], F32R) for n in range(2)]
        x = s.sb("x", [P, 2, D])
        y = s.sb("y", [P, 2, D])
        o = s.sb("o", [P, 2, D])
        gate = s.sb("gate", [P, 2, D])
        pick = s.sb("pick", [2, 2, P])
        frow = s.sb("frow", [1, D])
        fg = s.sb("fg", [P, D])
        st = s.sb("st", [P, 6, NT])
        acc = [s.ps(f"acc{n}", [P, D]) for n in range(2)]
        gps = s.ps("gps", [P, D])
        w_in = [s.sem(f"w_in{n}") for n in range(2)]
        w_hi, w_lo, f_in, pick_ok, gturn, g_ok = (s.sem(n) for n in ("w_hi", "w_lo", "f_in", "pick_ok", "gturn", "g_ok"))
        z_in = [s.sem(f"z_in{n}") for n in range(2)]
        x_in = [s.sem(f"x_in{n}") for n in range(2)]
        y_out = [s.sem(f"y_out{n}") for n in range(2)]
        full, yg, yr, sq, var, rs, nr, o_ok = (s.sem(n) for n in ("full", "yg", "yr", "sq", "var", "rs", "nr", "o_ok"))
        block = s.enter_context(nc.Block())
        wv = io["w_out"][0].rearrange("(k p) n -> p k n", p=P)
        W = [P] * NQ + [DEC]

        def store(act, t):
            n = W[t]
            act.wait_ge(o_ok, t + 1)
            dst = io["y_prompt"][0, t * P:t * P + n, :] if t < NQ else io["y_sample"][0]
            act.dma_start(dst, o[0:n, t % 2, :]).then_inc(y_out[t % 2], 16)

        @block.sync
        def _(sp):
            for t, n in enumerate(W):
                b = t % 2
                if t >= 2:
                    sp.wait_ge(full, t - 1)
                c0 = t * P
                sp.dma_start(raw(zh[b][:, :, 0:n]), dram["z"][0, :, :, c0:c0 + n].rearrange("k p c -> p k c")).then_inc(z_in[b], 16)
                sp.dma_start(raw(zl[b][:, :, 0:n]), dram["z"][1, :, :, c0:c0 + n].rearrange("k p c -> p k c")).then_inc(z_in[b], 16)
                if t >= 2:
                    sp.wait_ge(yr, 2 * (t - 1))
                sp.dma_start(x[0:n, b, :], io["x_prompt"][0, c0:c0 + n, :] if t < NQ else io["x_sample"][0]).then_inc(x_in[b], 16)

        @block.gpsimd
        def _(pool):
            pool.dma_start(frow[:, :], io["final_g"].rearrange("(a d) -> a d", a=1)).then_inc(f_in, 16)
            pool.memset(pick[:, :, :], 1.0).then_inc(pick_ok, 1)
            pool.wait_ge(pick_ok, 1)
            pool.affine_select(out=pick[:, :, :], in_=pick[:, :, :], compare_op=ALU.is_equal, fill=0.0, base=0,
                               pattern=[[-1, 2], [0, P]], channel_multiplier=1).then_inc(pick_ok, 1)

        @block.tensor
        def _(pe):
            pe.wait_ge(pick_ok, 2)
            for which in range(2):
                if which:
                    pe.wait_ge(g_ok, which)
                for n in range(2):
                    mm = pe.matmul(gps[:, n * 512:(n + 1) * 512], pick[:, which, :], keep["gate"][:, n * 512:(n + 1) * 512],
                                   start=True, stop=True)
                mm.then_inc(gturn, 1)
            pe.wait_ge(g_ok, 2)
            pe.wait_ge(f_in, 16)
            for n in range(2):
                mm = pe.matmul(gps[:, n * 512:(n + 1) * 512], pick[0:1, 0, :], frow[:, n * 512:(n + 1) * 512], start=True, stop=True)
            mm.then_inc(gturn, 1)
            for t, n in enumerate(W):
                b = t % 2
                pe.wait_ge(z_in[b], 32 * (t // 2 + 1))
                if t >= 2:
                    pe.wait_ge(yg, 2 * (t - 1))
                for k in range(KT):
                    if t == 0:
                        pe.wait_ge(w_lo, k + 1)
                    for m in range(2):
                        cols = slice(m * 512, (m + 1) * 512)
                        out = acc[b][0:n, cols]
                        pe.matmul(out, zh[b][:, k, 0:n], whi[:, k, cols], start=(k == 0), stop=False)
                        pe.matmul(out, zh[b][:, k, 0:n], wlo[:, k, cols], start=False, stop=False)
                        mm = pe.matmul(out, zl[b][:, k, 0:n], whi[:, k, cols], start=False, stop=(k == KT - 1))
                mm.then_inc(full, 1)

        @block.scalar
        def _(act):
            half = KT // 2
            for n in range(2):
                k = slice(n * half, (n + 1) * half)
                act.dma_start(wraw[:, k, :], wv[:, k, :]).then_inc(w_in[n], 16)
            for k in range(KT):
                if k % half == 0:
                    act.wait_ge(w_in[k // half], 16)
                act.activation(whi[:, k, :], wraw[:, k, :], ACT.Copy).then_inc(w_hi, 1)
            for n in range(3):
                act.wait_ge(gturn, n + 1)
                act.activation(fg[:, :] if n == 2 else gate[:, n, :], gps[:, :], ACT.Copy).then_inc(g_ok, 1)
            for t, n in enumerate(W):
                b = t % 2
                act.wait_ge(yr, 2 * (t + 1))
                if t >= 2:
                    act.wait_ge(y_out[b], 16 * (t // 2))
                act.activation(o[0:n, b, :], y[0:n, b, :], ACT.Square, accum_out=st[0:n, 0, t:t + 1]).then_inc(sq, 1)
                act.wait_ge(var, 2 * t + 2)
                act.activation(st[0:n, 3, t:t + 1], st[0:n, 2, t:t + 1], ACT.Sqrt).then_inc(rs, 1)
                if t >= 1:
                    store(act, t - 1)
            store(act, NT - 1)
            for n in range(2):
                act.wait_ge(y_out[n], 16 * len(W[n::2]))

        @block.vector
        def _(dve):
            for k in range(KT):
                dve.wait_ge(w_hi, k + 1)
                dve.tensor_tensor(wlo[:, k, :], wraw[:, k, :], raw(whi[:, k, :]), ALU.subtract).then_inc(w_lo, 1)

            def finish(t):
                n = W[t]
                r = [st[0:n, i, t:t + 1] for i in range(6)]
                dve.wait_ge(sq, t + 1)
                dve.tensor_scalar(r[1], r[0], 1.0 / D, EPS, ALU.mult, ALU.add).then_inc(var, 1)
                dve.wait_ge(var, 2 * t + 1)
                dve.reciprocal(r[2], r[1]).then_inc(var, 1)
                dve.wait_ge(rs, t + 1)
                dve.tensor_scalar(r[4], r[3], r[3], r[1], ALU.mult, ALU.mult).then_inc(nr, 1)
                dve.wait_ge(nr, 3 * t + 1)
                dve.tensor_scalar(r[5], r[4], -0.5, 1.5, ALU.mult, ALU.add).then_inc(nr, 1)
                dve.wait_ge(nr, 3 * t + 2)
                dve.tensor_scalar(r[4], r[5], r[3], None, ALU.mult).then_inc(nr, 1)
                dve.wait_ge(nr, 3 * t + 3)
                dve.scalar_tensor_tensor(out=o[0:n, t % 2, :], in0=y[0:n, t % 2, :], scalar=r[4], in1=fg[0:n, :],
                                         op0=ALU.mult, op1=ALU.mult).then_inc(o_ok, 1)

            dve.wait_ge(g_ok, 3)
            for t, n in enumerate(W):
                b = t % 2
                which = 0 if t < NQ else 1
                dve.wait_ge(full, t + 1)
                if t >= 2:
                    dve.wait_ge(o_ok, t - 1)
                for m in range(2):
                    cols = slice(m * 512, (m + 1) * 512)
                    dve.tensor_tensor(y[0:n, b, cols], acc[b][0:n, cols], gate[0:n, which, cols], ALU.mult).then_inc(yg, 1)
                dve.wait_ge(x_in[b], 16 * (t // 2 + 1))
                for m in range(2):
                    cols = slice(m * 512, (m + 1) * 512)
                    dve.wait_ge(yg, 2 * t + m + 1)
                    dve.tensor_tensor(y[0:n, b, cols], y[0:n, b, cols], x[0:n, b, cols], ALU.add).then_inc(yr, 1)
                if t >= 1:
                    finish(t - 1)
            finish(NT - 1)


_IN = ["x_prompt", "x_sample", "c_prompt", "c_sample", "cache_k", "cache_v", "cache_logf", "state_pool",
       "norm_g", "w_ada", "b_ada", "w_in", "b_f", "w_pool", "pool_scale", "w_out", "final_g"]
_OUT = [("y_prompt", (1, SEQ, D)), ("y_sample", (1, DEC, D)),
        ("k_prompt", (1, 1, SEQ, HEADS, DH)), ("v_prompt", (1, 1, SEQ, HEADS, DH)), ("logf_prompt", (1, 1, SEQ, HEADS)),
        ("pool_prompt", (1, 1, HIST, A)),
        ("k_sample", (1, 1, DEC, HEADS, DH)), ("v_sample", (1, 1, DEC, HEADS, DH)), ("logf_sample", (1, 1, DEC, HEADS)),
        ("pool_sample", (1, 1, HIST, A))]
_SCRATCH = {"v": [NQ + 2, P, HEADS * P], "k": [PAIRS, 2, P, TC], "q": [PAIRS, 2, P, T], "kf": [PAIRS, P, T],
            "u": [GROUPS, P, T], "pg": [GROUPS, P, T], "ag": [PAIRS, P, T], "d": [2, GROUPS, P, T],
            "fq": [HEADS, 4, TC], "fk": [HEADS, 4, TC], "z": [2, KT, P, T], "rden": [HEADS, T],
            "m": [HEADS, 2, T]}


def build(nc, io):
    dram = {n: nc.dram_tensor(f"scratch_{n}", s, F32, kind="Internal").ap() for n, s in _SCRATCH.items()}
    with Scope(nc, "keep") as s:
        keep = {
            "ident": s.sb("ident", [P, P]), "identb": s.sb("identb", [P, P], BF16), "mask": s.sb("mask", [P, P], BF16),
            "cols": s.sb("cols", [P, NROWS]), "bf": s.sb("bf", [HEADS, 1]), "gate": s.sb("gate", [2, D]),
            "shift": s.sb("shift", [P, KT, 2]), "scale": s.sb("scale", [P, KT, 2]),
        }
        stage_ada(nc, io, keep)
        stage_project(nc, io, keep, dram)
        stage_pool(nc, io, keep, dram)
        stage_attend(nc, io, keep, dram)
        stage_out(nc, io, keep, dram)


def kernel(**inputs):
    import concourse.bacc as bacc
    import numpy as np
    from concourse.bass_utils import run_bass_kernel_spmd

    nc = bacc.Bacc("TRN2", target_bir_lowering=False, num_devices=1)
    arrays, io = {}, {}
    for name in _IN:
        a = np.ascontiguousarray(inputs[name])
        arrays[f"in_{name}"] = a
        io[name] = nc.dram_tensor(f"in_{name}", a.shape, mybir.dt.from_np(a.dtype), kind="ExternalInput").ap()
    for name, shape in _OUT:
        io[name] = nc.dram_tensor(f"out_{name}", shape, F32, kind="ExternalOutput").ap()
    build(nc, io)
    r = run_bass_kernel_spmd(nc, [arrays], core_ids=[0])
    return tuple(r.results[0][f"out_{name}"] for name, _ in _OUT)
```
